# Optimizing a Trainium2 kernel written in Bass

```python
import math
import jax, jax.numpy as jnp
from jax import lax
import numpy as np

D_MODEL = 1024
BATCH = 1
SEQ = 1024
DEPTH = 2

S5_WIDTH = 256
S5_GROUP = 16
S5_GROUPS = S5_WIDTH // S5_GROUP
S5_STATE = 64
S5_DT_MIN = 0.001
S5_DT_MAX = 0.1

DSA_HEADS = 8
DSA_HEAD_DIM = 64
DSA_WIDTH = DSA_HEADS * DSA_HEAD_DIM
DSA_KV_DIM = 64
IDX_HEADS = 4
IDX_DIM = 64
DSA_TOPK_MAX = 256
Q_BLOCK = 128

RET_HEADS = 4
RET_HEAD_DIM = 64
RET_WIDTH = RET_HEADS * RET_HEAD_DIM
RET_CHUNK = 128
ROPE_BASE = 10000.0

REL_BUCKETS = 32
REL_MAX_DIST = 128

D_FF = ((8 * D_MODEL // 3 + 255) // 256) * 256
MIX_WIDTH = S5_WIDTH + DSA_WIDTH + RET_WIDTH

IN_SPLITS = (S5_WIDTH,
             DSA_WIDTH, DSA_KV_DIM, DSA_KV_DIM,
             IDX_HEADS * IDX_DIM, IDX_DIM, IDX_HEADS,
             RET_WIDTH, RET_WIDTH, RET_WIDTH, RET_WIDTH)
IN_WIDTH = sum(IN_SPLITS)

RMS_EPS = 1e-6
GN_EPS = 1e-6
NEG_INF = -1e30

kernel_name = "hybrid_s5_dsa_retention_trunk"

def rmsnorm(x, g):
    xf = x.astype(jnp.float32)
    y = xf * lax.rsqrt(jnp.mean(xf * xf, axis=-1, keepdims=True) + RMS_EPS)
    return (y * g.astype(jnp.float32)).astype(x.dtype)

def t5_bucket(dist):
    n = jnp.maximum(dist, 0)
    max_exact = REL_BUCKETS // 2
    nf = jnp.maximum(n, 1).astype(jnp.float32)
    large = max_exact + (jnp.log(nf / max_exact) / math.log(REL_MAX_DIST / max_exact)
                         * (REL_BUCKETS - max_exact)).astype(jnp.int32)
    large = jnp.minimum(large, REL_BUCKETS - 1)
    return jnp.where(n < max_exact, n, large)

def rotary(x, pos):
    half = x.shape[-1] // 2
    inv = ROPE_BASE ** (-jnp.arange(half, dtype=jnp.float32) / half)
    ang = pos.astype(jnp.float32)[:, None] * inv[None, :]
    cos = jnp.cos(ang)[None, :, None, :]
    sin = jnp.sin(ang)[None, :, None, :]
    x1, x2 = x[..., :half], x[..., half:]
    return jnp.concatenate([x1 * cos - x2 * sin, x2 * cos + x1 * sin], axis=-1)

def s5_mixer(u, a_re, a_im, log_dt, b_re, b_im, c_re, c_im, d_skip, glu_w, glu_b):
    bsz, seq, _ = u.shape
    f32 = jnp.float32
    uf = u.astype(f32).reshape(bsz, seq, S5_GROUPS, S5_GROUP)
    ar, ai = a_re.astype(f32), a_im.astype(f32)
    dt = jnp.exp(log_dt.astype(f32))[:, None]
    mag = jnp.exp(ar * dt)
    ang = ai * dt
    abr, abi = mag * jnp.cos(ang), mag * jnp.sin(ang)
    den = ar * ar + ai * ai
    nr, ni = abr - 1.0, abi
    cr = (nr * ar + ni * ai) / den
    ci = (ni * ar - nr * ai) / den
    br, bi = b_re.astype(f32), b_im.astype(f32)
    bbr = cr[..., None] * br - ci[..., None] * bi
    bbi = cr[..., None] * bi + ci[..., None] * br
    xr = jnp.einsum('blgp,gnp->blgn', uf, bbr)
    xi = jnp.einsum('blgp,gnp->blgn', uf, bbi)
    a_r = jnp.broadcast_to(abr, (1, seq, S5_GROUPS, S5_STATE))
    a_i = jnp.broadcast_to(abi, (1, seq, S5_GROUPS, S5_STATE))

    def combine(e1, e2):
        a1r, a1i, b1r, b1i = e1
        a2r, a2i, b2r, b2i = e2
        return (a2r * a1r - a2i * a1i,
                a2r * a1i + a2i * a1r,
                a2r * b1r - a2i * b1i + b2r,
                a2r * b1i + a2i * b1r + b2i)

    _, _, hr, hi = lax.associative_scan(combine, (a_r, a_i, xr, xi), axis=1)
    y = (jnp.einsum('blgn,gpn->blgp', hr, c_re.astype(f32))
         - jnp.einsum('blgn,gpn->blgp', hi, c_im.astype(f32))
         + d_skip.astype(f32)[None, None] * uf)
    y = jax.nn.gelu(y.reshape(bsz, seq, S5_WIDTH))
    y = y * jax.nn.sigmoid(y @ glu_w.astype(f32) + glu_b.astype(f32))
    return y.astype(u.dtype)

def dsa_attention(q, k, v, q_idx, k_idx, w_idx, rel_bias):
    f32 = jnp.float32
    bsz, seq = q.shape[0], q.shape[1]
    k_sel = min(DSA_TOPK_MAX, seq // 4)
    n_blk = seq // Q_BLOCK

    def to_blocks(a):
        return jnp.swapaxes(a.reshape((bsz, n_blk, Q_BLOCK) + a.shape[2:]), 0, 1)

    kidx = k_idx.astype(f32)
    key_pos = jnp.arange(seq, dtype=jnp.int32)
    scale = DSA_HEAD_DIM ** -0.5

    def block(args):
        qb, qib, wb, start = args
        q_pos = start + jnp.arange(Q_BLOCK, dtype=jnp.int32)
        dots = jnp.einsum('bqhd,bsd->bqhs', qib.astype(f32), kidx) * (IDX_DIM ** -0.5)
        score = jnp.einsum('bqhs,bqh->bqs', jax.nn.relu(dots), wb.astype(f32)) * (IDX_HEADS ** -0.5)
        causal = key_pos[None, None, :] <= q_pos[None, :, None]
        score = jnp.where(causal, score, NEG_INF)
        _, sel = lax.top_k(score, k_sel)
        flat = sel.reshape(bsz, Q_BLOCK * k_sel, 1)
        kg = jnp.take_along_axis(k, flat, axis=1).reshape(bsz, Q_BLOCK, k_sel, DSA_KV_DIM)
        vg = jnp.take_along_axis(v, flat, axis=1).reshape(bsz, Q_BLOCK, k_sel, DSA_KV_DIM)
        dist = q_pos[None, :, None] - sel
        bias = jnp.moveaxis(rel_bias[t5_bucket(dist)], -1, 2)
        logits = (jnp.einsum('bqhd,bqkd->bqhk', qb, kg).astype(f32) * scale
                  + bias.astype(f32))
        logits = jnp.where((dist >= 0)[:, :, None, :], logits, NEG_INF)
        p = jax.nn.softmax(logits, axis=-1).astype(v.dtype)
        return jnp.einsum('bqhk,bqkd->bqhd', p, vg)

    starts = jnp.arange(n_blk, dtype=jnp.int32) * Q_BLOCK
    out = lax.map(block, (to_blocks(q), to_blocks(q_idx), to_blocks(w_idx), starts))
    return jnp.swapaxes(out, 0, 1).reshape(bsz, seq, DSA_WIDTH)

def retention(q, k, v, g, gn_w):
    f32 = jnp.float32
    bsz, seq, _ = q.shape
    nc = seq // RET_CHUNK
    pos = jnp.arange(seq, dtype=jnp.int32)
    shp = (bsz, seq, RET_HEADS, RET_HEAD_DIM)
    qf = rotary(q.astype(f32).reshape(shp), pos)
    kf = rotary(k.astype(f32).reshape(shp), pos) * (RET_HEAD_DIM ** -0.5)
    vf = v.astype(f32).reshape(shp)
    cshp = (bsz, nc, RET_CHUNK, RET_HEADS, RET_HEAD_DIM)
    qc, kc, vc = qf.reshape(cshp), kf.reshape(cshp), vf.reshape(cshp)

    gamma = 1.0 - 2.0 ** (-5.0 - jnp.arange(RET_HEADS, dtype=f32))
    log_g = jnp.log(gamma)
    i = jnp.arange(RET_CHUNK, dtype=f32)
    diff = i[:, None] - i[None, :]
    decay = jnp.where(diff >= 0, jnp.exp(log_g[:, None, None] * jnp.maximum(diff, 0.0)), 0.0)

    qk = jnp.einsum('bnihd,bnjhd->bnhij', qc, kc) * decay[None, None]
    inner = jnp.einsum('bnhij,bnjhd->bnihd', qk, vc)

    wk = jnp.exp(log_g[:, None] * (RET_CHUNK - 1.0 - i)[None, :])
    kv = jnp.einsum('bnjhd,hj,bnjhe->bnhde', kc, wk, vc)
    g_chunk = jnp.exp(log_g * RET_CHUNK)[None, :, None, None]

    def step(state, kv_n):
        return g_chunk * state + kv_n, state

    init = jnp.zeros((bsz, RET_HEADS, RET_HEAD_DIM, RET_HEAD_DIM), f32)
    _, prev = lax.scan(step, init, jnp.swapaxes(kv, 0, 1))
    prev = jnp.swapaxes(prev, 0, 1)
    wq = jnp.exp(log_g[:, None] * (i + 1.0)[None, :])
    cross = jnp.einsum('bnihd,bnhde->bnihe', qc, prev) * wq.T[None, None, :, :, None]
    o = (inner + cross).reshape(shp)

    mu = jnp.mean(o, axis=-1, keepdims=True)
    var = jnp.mean(jnp.square(o - mu), axis=-1, keepdims=True)
    o = ((o - mu) * lax.rsqrt(var + GN_EPS)).reshape(bsz, seq, RET_WIDTH) * gn_w.astype(f32)
    return (jax.nn.silu(g.astype(f32)) * o).astype(q.dtype)

def setup_inputs(seed: int = 0) -> dict:
    key = jax.random.key(seed)
    ks = jax.random.split(key, 24)
    f32 = jnp.float32
    nrm = lambda k, s: jax.random.normal(k, s, f32)
    G, N, P = S5_GROUPS, S5_STATE, S5_GROUP
    lo, hi = math.log(S5_DT_MIN), math.log(S5_DT_MAX)
    return {
        "x": nrm(ks[0], (BATCH, SEQ, D_MODEL)),
        "w_in": nrm(ks[1], (DEPTH, D_MODEL, IN_WIDTH)) * D_MODEL ** -0.5,
        "w_out": nrm(ks[2], (DEPTH, MIX_WIDTH, D_MODEL)) * MIX_WIDTH ** -0.5,
        "norm_mix": 1.0 + 0.02 * nrm(ks[3], (DEPTH, D_MODEL)),
        "ssm_a_re": -0.5 + 0.01 * nrm(ks[4], (DEPTH, G, N)),
        "ssm_a_im": math.pi * jnp.arange(N, dtype=f32)[None, None, :] + 0.01 * nrm(ks[5], (DEPTH, G, N)),
        "ssm_log_dt": lo + (hi - lo) * jax.random.uniform(ks[6], (DEPTH, G), f32),
        "ssm_b_re": nrm(ks[7], (DEPTH, G, N, P)) * (2.0 * P) ** -0.5,
        "ssm_b_im": nrm(ks[8], (DEPTH, G, N, P)) * (2.0 * P) ** -0.5,
        "ssm_c_re": nrm(ks[9], (DEPTH, G, P, N)) * (2.0 * N) ** -0.5,
        "ssm_c_im": nrm(ks[10], (DEPTH, G, P, N)) * (2.0 * N) ** -0.5,
        "ssm_d": nrm(ks[11], (DEPTH, G, P)),
        "ssm_glu_w": nrm(ks[12], (DEPTH, S5_WIDTH, S5_WIDTH)) * S5_WIDTH ** -0.5,
        "ssm_glu_b": 0.01 * nrm(ks[13], (DEPTH, S5_WIDTH)),
        "rel_bias": 0.5 * nrm(ks[14], (REL_BUCKETS, DSA_HEADS)),
        "ret_gn": 1.0 + 0.02 * nrm(ks[15], (DEPTH, RET_WIDTH)),
        "norm_ffn": 1.0 + 0.02 * nrm(ks[16], (DEPTH, D_MODEL)),
        "w_ffn_in": nrm(ks[17], (DEPTH, D_MODEL, 2 * D_FF)) * D_MODEL ** -0.5,
        "w_ffn_out": nrm(ks[18], (DEPTH, D_FF, D_MODEL)) * D_FF ** -0.5,
        "norm_final": 1.0 + 0.02 * nrm(ks[19], (D_MODEL,)),
    }

def reference(x, w_in, w_out, norm_mix, ssm_a_re, ssm_a_im, ssm_log_dt, ssm_b_re, ssm_b_im,
              ssm_c_re, ssm_c_im, ssm_d, ssm_glu_w, ssm_glu_b, rel_bias, ret_gn,
              norm_ffn, w_ffn_in, w_ffn_out, norm_final):
    bsz, seq, _ = x.shape
    split_pts = [int(s) for s in np.cumsum(IN_SPLITS)[:-1]]
    for l in range(DEPTH):
        h = rmsnorm(x, norm_mix[l])
        proj = h @ w_in[l]
        (u, dq, dk, dv, iq, ik, iw, rq, rk, rv, rg) = jnp.split(proj, split_pts, axis=-1)
        y_a = s5_mixer(u, ssm_a_re[l], ssm_a_im[l], ssm_log_dt[l], ssm_b_re[l], ssm_b_im[l],
                       ssm_c_re[l], ssm_c_im[l], ssm_d[l], ssm_glu_w[l], ssm_glu_b[l])
        y_b = dsa_attention(dq.reshape(bsz, seq, DSA_HEADS, DSA_HEAD_DIM), dk, dv,
                            iq.reshape(bsz, seq, IDX_HEADS, IDX_DIM), ik, iw, rel_bias)
        y_c = retention(rq, rk, rv, rg, ret_gn[l])
        mix = jnp.concatenate([y_a, y_b.astype(x.dtype), y_c], axis=-1)
        x = x + mix @ w_out[l]
        h = rmsnorm(x, norm_ffn[l])
        gate, up = jnp.split(h @ w_ffn_in[l], 2, axis=-1)
        x = x + (jax.nn.silu(gate) * up) @ w_ffn_out[l]
    return rmsnorm(x, norm_final)


_drawn_inputs = setup_inputs


def setup_inputs(seed=0):
    import zlib

    import numpy as np

    out = dict(_drawn_inputs(seed))
    spreads = {}
    factors = {'ssm_a_re': 64.0,
     'ssm_a_im': 24.32,
     'ssm_log_dt': 200.0,
     'ssm_b_re': 32.616,
     'ssm_b_im': 33.512,
     'ssm_c_re': 32.768,
     'ssm_c_im': 33.16,
     'ssm_glu_b': 64.0,
     'ret_gn': 5.481,
     'norm_final': 22.936,
     'norm_ffn': 3.91}
    for name, (base, spread) in spreads.items():
        noise = np.random.default_rng([zlib.crc32(name.encode()), seed]).standard_normal(out[name].shape)
        drawn = base * np.exp(spread * noise) if base else spread * noise
        out[name] = __import__('jax').numpy.asarray(drawn.astype(out[name].dtype))
    for name, factor in factors.items():
        out[name] = (out[name] * factor).astype(out[name].dtype)
    return out
```

```python
from contextlib import ExitStack, contextmanager

import numpy as np

import concourse.bass as bass
from concourse import mybir

ALU = mybir.AluOpType
ACTF = mybir.ActivationFunctionType
F32 = mybir.dt.float32
F32R = mybir.dt.float32r
BF16 = mybir.dt.bfloat16
AX_X = mybir.AxisListType.X
ds = bass.ds

P = 128
T, D, DEPTH = 1024, 1024, 2
HALF = 512
KT = D // P
TT = HALF // P
NB = T // P
D_FF = 2816
FT = D_FF // P
FF_CHUNKS = (8, 8, 6)
TOPK = 256
HEADS, DH = 8, 64
IDX_HEADS = 4
RH = 4
BUCKETS = 32
EPS = 1e-6
NONCAUSAL = -1e38
TAKEN = -3e38
MASKED = -1e31
S5_STEPS = 8
S5_CHUNKS = T // S5_STEPS

C_U, C_Q, C_K, C_V, C_IQ, C_IK, C_IW, C_RET = 0, 256, 768, 832, 896, 1152, 1216, 1220
CM_U, CM_Q, CM_IQ, CM_K, CM_IK, CM = 0, 2, 6, 8, 9, 10

UNITS_PROJ = CM + 1 + 8
UNITS_OUT = 8
UNITS_FFN = 3 * FT
UNITS = 2 * (UNITS_PROJ + UNITS_OUT + UNITS_FFN)

GROUPS = {"A": (0, 1), "B": (1, 1), "C": (2, 2), "D": (4, 2), "E": (6, 1), "F": (7, 1)}

PER_LAYER = {
    "A_free": 131, "A_to_act": 53, "A_to_dve": 8, "B_free": 123, "B_to_act": 5, "B_to_dve": 48, "C_free": 62,
    "C_to_act": 22, "C_to_dve": 32, "D_free": 64, "D_to_act": 24, "D_to_dve": 32, "E_free": 30, "E_to_act": 1,
    "E_to_dve": 19, "F_free": 31, "F_to_act": 9, "F_to_dve": 10, "a_ready": 44, "act_chain": 33,
    "angle_ready": 1, "ao_ready": 8, "cm_ready": 2, "dt_ready": 1, "dve_chain": 847, "gate_ready": 44,
    "gate_used": 44, "gstd_ready": 2, "gvar_ready": 2, "h_hi_ready": 32, "h_ready": 32, "hi_ready": 186,
    "hprev_ready": 2, "kt_ready": 2, "mask_ready": 6, "mean_ready": 4, "mix_hi_ready": 10, "mix_ready": 10,
    "nmax_ready": 64, "norm_tmp": 32, "o_ready": 2, "p_ready": 64, "params_loaded": 192, "s5_loaded": 128, "ptA_ready": 48,
    "ptB_ready": 48, "qs_ready": 2, "rT_ready": 2, "raw_loaded0": 1536, "raw_loaded1": 1536, "relu_ready": 24,
    "relu_used": 24, "ret_in": 2, "ret_out": 2, "rot_ready": 2, "rstd_ready": 4, "sig_ready": 1,
    "square_ready": 32, "square_summed": 32, "st_ready": 8, "state_ready": 8, "trig_ready": 1, "unit_done": 186,
    "v_ready": 2, "vt_ready": 2, "weights_ready": 186, "x_loaded": 64, "x_stored": 32, "x_updated": 4,
    "y_gated": 1, "y_ready": 2, "z_ready": 2,
}

WRONG = []

CREDIT = {"unit_done": 2, "weights_ready": 2, "relu_used": 2, "gate_used": 1, "layer_done": 1}
CREDIT.update({f"{g}_free": 1 for g in GROUPS})


class Counts:

    def __init__(self, eng, name, held=None):
        self.eng, self.name, self.held = eng, name, held
        self.count = {}
        self.loops = []

    def value(self, sem, n):
        v = n + CREDIT.get(sem, 0)
        for reg, per in self.loops:
            if per.get(sem, 0):
                v = reg * per[sem] + v
        return v

    def add(self, sem, n=1):
        self.count[sem] = self.count.get(sem, 0) + n
        return self.count[sem]

    def seen(self, sem, n=1):
        return self.value(sem, self.add(sem, n))

    def taken(self, sem):
        return self.value(sem, self.add(sem)) - CREDIT[sem]

    def made(self, sem, n=1):
        self.add(sem, n)
        return n

    def now(self, sem):
        return self.value(sem, self.count[sem])

    @contextmanager
    def loop(self, times, **per):
        before = dict(self.count)
        if self.held is not None:
            self.eng.sem_inc(self.held, 1)
        with self.eng.Fori(0, times) as i:
            self.loops.append((i, per))
            yield i
            self.loops.pop()
        did = {s: n - before.get(s, 0) for s, n in self.count.items() if n != before.get(s, 0)}
        assert did == {s: n for s, n in per.items() if n}, (self.name, did, per)
        for s, n in per.items():
            self.count[s] += n * (times - 1)

    @contextmanager
    def layers(self):
        before = dict(self.count)
        with self.eng.Fori(0, DEPTH) as l:
            self.loops.append((l, PER_LAYER))
            yield l
            self.loops.pop()
        for s in list(self.count):
            n = self.count[s] - before.get(s, 0)
            if PER_LAYER.get(s, 0) != n:
                WRONG.append((self.name, s, n, PER_LAYER.get(s)))
            self.count[s] += n * (DEPTH - 1)


def constants():
    f = np.float32
    parts = {}
    parts["ident"] = np.eye(P, dtype=f)
    parts["ones"] = np.ones((P, P), f)
    parts["noncausal"] = np.triu(np.full((P, P), NONCAUSAL, f), 1)
    parts["quads"] = np.kron(np.eye(4, dtype=f), np.ones((32, 32), f))
    inv = (f(10000.0) ** (-np.arange(32, dtype=f) / f(32))).astype(f)
    ang = (np.arange(T, dtype=f)[:, None] * inv[None, :]).astype(f).astype(np.float64)
    for n, fn in (("cos", np.cos), ("sin", np.sin)):
        parts[n] = fn(ang).astype(f).reshape(NB, P, 32).transpose(1, 0, 2).reshape(P, NB * 32)
    gamma = 1.0 - 2.0 ** (-5.0 - np.arange(RH, dtype=np.float64))
    lg = np.log(gamma)
    i = np.arange(P, dtype=np.float64)
    diff = i[None, :] - i[:, None]
    dec = np.where(diff[None] >= 0, np.exp(lg[:, None, None] * np.maximum(diff, 0.0)[None]), 0.0)
    parts["decay"] = (dec * 0.125).astype(f).transpose(1, 0, 2).reshape(P, RH * P)
    parts["wk"] = (np.exp(lg[None, :] * (P - 1.0 - i)[:, None]) * 0.125).astype(f)
    wq = np.exp(lg[:, None] * (i + 1.0)[None, :])
    parts["wq"] = np.stack([np.repeat(wq[2 * t:2 * t + 2], 64, axis=0) for t in range(2)], 1).astype(f).reshape(P, 2 * P)
    gc = np.exp(lg * P)
    parts["gchunk"] = np.stack([np.repeat(gc[2 * t:2 * t + 2], 64) for t in range(2)], 1).astype(f)
    dist = np.maximum(255 - np.arange(384), 0)
    nf = np.maximum(dist, 1).astype(f)
    large = 16 + (np.log(nf / f(16)).astype(f) / f(np.log(8.0)) * f(16)).astype(np.int32)
    bucket = np.where(dist < 16, dist, np.minimum(large, BUCKETS - 1))
    hot = np.zeros((P, 384), f)
    hot[bucket, np.arange(384)] += 1.0
    hot[BUCKETS - 1, :] -= 1.0
    parts["buckets"] = hot
    at, n = {}, 0
    for k, a in parts.items():
        at[k] = (n, a.shape[1])
        n += a.shape[1]
    return np.ascontiguousarray(np.concatenate(list(parts.values()), 1)), at


def build_trunk(nc, x, w_in, w_out, norm_mix, a_re, a_im, log_dt, b_re, b_im, c_re, c_im, ssm_d, glu_w,
                glu_b, rel_bias, ret_gn, norm_ffn, w_ffn_in, w_ffn_out, norm_final, const, out, at):
    ctx = ExitStack()
    with ctx:
        def sb(name, shape, dt=F32, where=None):
            return (where or ctx).enter_context(nc.sbuf_tensor(name, shape, dt))

        cst = sb("cst", [P, const.shape[1]])

        def table(name):
            o, n = at[name]
            return cst[:, o:o + n]

        ident = table("ident")
        h_hi = sb("h_hi", [P, KT, HALF], F32R)
        h_lo = sb("h_lo", [P, KT, HALF], F32R)
        w_raw = sb("w_raw", [P, 2, 1024])
        w_hi = sb("w_hi", [P, 2, 1024], F32R)
        w_lo = sb("w_lo", [P, 2, 1024], F32R)
        cm = sb("cm", [P, CM - 2, T])
        iq = sb("iq", [P, 2, HALF])
        vw = sb("vw", [P, NB, P])
        ret_T = sb("ret_T", [P, 2, T])
        x_T = sb("x_T", [P, KT, HALF])
        bias_win = sb("bias_win", [P, HEADS, 256])
        NK = [P * (b + 1) for b in range(NB)]
        score = {b: sb(f"score{b}", [P, NK[b]]) for b in (2, 3)}
        ident_b = sb("ident_b", [P, P], BF16)
        causal_b = sb("causal_b", [P, P], BF16)
        gains = sb("gains", [P, 2, KT])
        gain_last = sb("gain_last", [P, KT])
        gn_row = sb("gn_row", [P, 256])
        s5p = sb("s5p", [P, 64, 8])
        s5_glu = sb("s5_glu", [P, 2, 256])
        s5_col = sb("s5_col", [P, 2, 2])
        rel_b = sb("rel_b", [BUCKETS, HEADS])
        top8 = sb("top8", [P, 8])
        nmax = sb("nmax", [P, HEADS])
        rsum = sb("rsum", [P, HEADS])
        rinv = sb("rinv", [P, HEADS])
        gsum = sb("gsum", [P, 4, TT * RH])
        state = sb("state", [P, 2, 2, 64])

        def shared(size, *stages):
            got = {}
            for tensors in stages:
                with ExitStack() as stage:
                    for name, shape, dt in tensors:
                        got[name] = sb(name, shape, dt, stage)
            sb(f"shared{size}", [P, size])
            return got

        big = shared(
            11776,
            [("a_hi", [P, 8, HALF], F32R), ("a_lo", [P, 8, HALF], F32R)]
            + [(f"score{b}", [P, NK[b]], F32) for b in range(4, NB)],
            [("r_in", [P, TT, 4, 256], F32), ("rot", [P, TT, 2, 256], F32), ("rtmp", [P, 2, 1024], F32),
             ("rqT", [P, 2, HALF], F32), ("rkT", [P, 2, HALF], F32)],
            [("Z", [P, 2, 8, 4, 32], F32), ("Vt", [P, 8, 2, P], F32), ("Yt", [P, 2, 8, 4, 32], F32),
             ("Kt", [P, 8, P], F32), ("Et", [P, 2, 4, P], F32), ("Gt", [P, 2, 4, P], F32),
             ("Ht", [P, 2, 4, P], F32), ("Xt", [P, 2, 512], F32)],
            [("prob", [P, 2, 1024], F32), ("probT", [P, 2, 1024], F32), ("ao", [P, 512], F32)],
            [("xtok", [P, 2, D], F32), ("brow", [HEADS, 384], F32)],
        )
        small = shared(
            2560,
            [("sq", [P, 2, HALF], F32), ("ntmp", [P, 2, HALF], F32), ("rstd", [P, HALF], F32)],
            [("relu", [P, 2, 1024], F32)],
            [("s5_b", [P, 2, 8, 16], F32), ("s5_c", [P, 2, 2, P], F32), ("s5_ct", [P, 2, 8, 32], F32),
             ("s5_bb", [P, 2, 8, 16], F32), ("s5_t", [P, 2, 8, 16], F32)],
            [("gate", [P, HALF], F32), ("atmp", [P, HALF], F32)],
        )
        a_hi, a_lo = big["a_hi"], big["a_lo"]
        score.update({b: big[f"score{b}"] for b in range(4, NB)})
        r_in, rot, rtmp, rqT, rkT = (big[n] for n in ("r_in", "rot", "rtmp", "rqT", "rkT"))
        Z, Vt, Yt, Kt, Et, Gt, Ht, Xt = (big[n] for n in ("Z", "Vt", "Yt", "Kt", "Et", "Gt", "Ht", "Xt"))
        prob, probT, ao, xtok, brow = (big[n] for n in ("prob", "probT", "ao", "xtok", "brow"))
        sq, ntmp, rstd, relu = (small[n] for n in ("sq", "ntmp", "rstd", "relu"))
        s5_b, s5_c, s5_ct, s5_bb, s5_t = (small[n] for n in ("s5_b", "s5_c", "s5_ct", "s5_bb", "s5_t"))
        gate, atmp = small["gate"], small["atmp"]

        psum = ctx.enter_context(nc.psum_tensor("psum", [P, 4096], F32))
        x_dram = nc.dram_tensor("x_half", [2, P, KT * HALF], F32).ap()
        bias_dram = nc.dram_tensor("bias_rows", [HEADS, P, 384], F32).ap()

        def bank(group, a=0, b=None):
            first, n = GROUPS[group]
            return psum[:, first * 512 + a:first * 512 + (n * 512 if b is None else b)]

        names = ["raw_loaded0", "raw_loaded1", "hi_ready", "weights_ready", "unit_done", "square_ready", "square_summed",
                 "mean_ready", "rstd_ready", "norm_tmp", "h_hi_ready", "h_ready", "x_loaded", "x_stored",
                 "x_updated", "params_loaded", "s5_loaded", "layer_done", "const_loaded", "xtok_loaded0", "xtok_loaded1", "bias_stored",
                 "bias_loaded", "ident_ready", "cm_ready", "vw_ready", "ret_in", "relu_ready", "relu_used",
                 "score_ready", "mask_ready", "nmax_ready", "p_ready", "ptA_ready", "ptB_ready", "ao_ready",
                 "mix_hi_ready", "mix_ready", "gate_ready", "gate_used", "a_ready", "out_stored0", "out_stored1",
                 "rot_ready", "rT_ready", "qs_ready", "st_ready", "o_ready", "state_ready", "gvar_ready",
                 "gstd_ready", "ret_out", "retT_ready", "silu_ready", "dt_ready", "angle_ready",
                 "trig_ready", "ct_ready", "z_ready", "vt_ready", "v_ready", "hprev_ready", "kt_ready",
                 "y_ready", "sig_ready", "y_gated", "xtok_used", "fin_ready", "fin_out",
                 "sp_chain", "act_chain", "dve_chain", "pool_chain", "pe_chain", "dve_held", "pe_held"]
        for g in GROUPS:
            names += [f"{g}_free", f"{g}_to_act", f"{g}_to_dve"]
        sems = {n: ctx.enter_context(nc.semaphore(n)) for n in names}
        block = ctx.enter_context(nc.Block())

        rows = w_in.rearrange("l (k p) c -> p l k c", p=P)
        rows_out = w_out.rearrange("l (k p) c -> p l k c", p=P)
        rows_gu = w_ffn_in.rearrange("l (k p) c -> p l k c", p=P)
        rows_down = w_ffn_out.rearrange("l (k p) c -> p l k c", p=P)


        @block.sync
        def _(eng):
            st = Counts(eng, "sp")
            eng.dma_start(cst[:, :], const).then_inc(sems["const_loaded"], 16)
            eng.dma_start(gain_last[:, :], norm_final.rearrange("(k p) -> p k", p=P),
                          allow_slow_non_contiguous=True).then_inc(
                sems["const_loaded"], 16)
            eng.dma_start(rel_b[:, :], rel_bias).then_inc(sems["const_loaded"], 16)

            def load_unit(width, *sources):
                u = st.add("weights_ready") - 1
                eng.wait_ge(sems["weights_ready"], st.value("weights_ready", u + 1) - 2)
                dst = w_raw[:, u % 2, :].rearrange("p (k c) -> p k c", c=width)
                a = 0
                for src in sources:
                    w = src.shape[-1]
                    ins = eng.dma_start(dst[:, :, a:a + w], src.rearrange("p l k c -> p (l k) c"))
                    ins.then_inc(sems[f"raw_loaded{u % 2}"], st.made(f"raw_loaded{u % 2}", 16))
                    a += w

            def proj(l):
                with st.loop(3, weights_ready=2, raw_loaded0=16, raw_loaded1=16) as i:
                    for e in range(2):
                        load_unit(P, rows[:, ds(l, 1), :, ds(i * 256 + e * P, P)])
                for e in range(2):
                    load_unit(P, rows[:, ds(l, 1), :, C_IQ + e * P:C_IQ + (e + 1) * P])
                for c in (C_K, C_IK):
                    one = rows[:, ds(l, 1), :, c:c + 64]
                    load_unit(P, one, one)
                load_unit(P, rows[:, ds(l, 1), :, C_V:C_V + 64], rows[:, ds(l, 1), :, C_IW:C_IW + 64])
                for n in range(2):
                    for j in range(4):
                        c = C_RET + n * 512
                        load_unit(512, rows[:, ds(l, 1), 2 * j:2 * j + 2, c:c + 512])

            def mix_out(l):
                with st.loop(4, weights_ready=2, raw_loaded0=16, raw_loaded1=16) as i:
                    for e in range(2):
                        load_unit(P, rows_out[:, ds(l, 1), :, ds(i * 256 + e * P, P)])

            def ffn(l):
                f0 = 0
                for n in FF_CHUNKS:
                    with st.loop(n, weights_ready=2, raw_loaded0=16, raw_loaded1=16) as i:
                        load_unit(P, rows_gu[:, ds(l, 1), :, ds(i * P + f0 * P, P)])
                        load_unit(P, rows_gu[:, ds(l, 1), :, ds(i * P + (D_FF + f0 * P), P)])
                    with st.loop(n // 2, weights_ready=2, raw_loaded0=16, raw_loaded1=16) as i:
                        for e in range(2):
                            load_unit(D, rows_down[:, ds(l, 1), ds(i * 2 + (f0 + e), 1), :])
                    f0 += n

            with st.layers() as l:
                eng.wait_ge(sems["layer_done"], l + 1)

                def par(dst, src):
                    eng.dma_start(dst, src, allow_slow_non_contiguous=True).then_inc(sems["params_loaded"], st.made("params_loaded", 16))

                lay = ds(l, 1)
                par(gains[:, 0, :], norm_mix[lay, :].rearrange("l (k p) -> p (l k)", p=P))
                par(gains[:, 1, :], norm_ffn[lay, :].rearrange("l (k p) -> p (l k)", p=P))
                par(gn_row[:, :], ret_gn[lay, :].to_broadcast([P, 256]))
                par(s5_glu[:, :, :], glu_w[lay, :, :].rearrange("l (k p) c -> p (l k) c", p=P))
                par(s5_col[:, 0, :], ssm_d[lay, :, :].rearrange("l (h g) p -> (l g p) h", h=2))
                par(s5_col[:, 1, :], glu_b[lay, :].rearrange("l (h p) -> p (l h)", h=2))
                for r in range(2):
                    half = slice(64 * r, 64 * r + 64)
                    par(s5p[half, 0, :], a_re[lay, r::2, :].rearrange("l q n -> n (l q)"))
                    par(s5p[half, 1, :], a_im[lay, r::2, :].rearrange("l q n -> n (l q)"))
                    par(s5p[half, 2, :], log_dt[lay, r::2].to_broadcast([64, 8]))
                for h in range(2):
                    proj(l)
                for h in range(2):
                    mix_out(l)
                    ffn(l)

        @block.gpsimd
        def _(eng):
            st = Counts(eng, "pool")
            eng.wait_ge(sems["const_loaded"], 48)
            with st.layers():
                with st.loop(UNITS // 2, hi_ready=2, weights_ready=2):
                    for s in range(2):
                        eng.wait_ge(sems["hi_ready"], st.seen("hi_ready"))
                        eng.tensor_tensor(
                            w_lo[:, s, :], w_raw[:, s, :], w_hi[:, s, :].bitcast(F32), ALU.subtract).then_inc(sems["weights_ready"], st.made("weights_ready"))

        @block.scalar
        def _(eng):
            st = Counts(eng, "act")

            def link(ins):
                ins.then_inc(sems["act_chain"], st.made("act_chain"))
                eng.wait_ge(sems["act_chain"], st.now("act_chain"))

            act = eng.activation

            def prep(pieces=1):
                u = st.add("hi_ready") - 1
                eng.wait_ge(sems["unit_done"], st.value("unit_done", u + 1) - 2)
                eng.wait_ge(sems[f"raw_loaded{u % 2}"], st.seen(f"raw_loaded{u % 2}", 16 * pieces))
                ins = act(w_hi[:, u % 2, :], w_raw[:, u % 2, :], ACTF.Copy)
                ins.then_inc(sems["hi_ready"], 1)

            def load_x(h):
                eng.dma_start(
                    x_T[:, :, :], x_dram[h].rearrange("p (k c) -> p k c", k=KT)).then_inc(sems["x_loaded"], st.made("x_loaded", 16))

            def store_x(h):
                eng.dma_start(
                    x_dram[h].rearrange("p (k c) -> p k c", k=KT), x_T[:, :, :]).then_inc(sems["x_stored"], st.made("x_stored", 16))
                eng.wait_ge(sems["x_stored"], st.value("x_stored", st.count["x_stored"]))

            def norm(final=False):
                for k in range(KT):
                    if k >= 2:
                        eng.wait_ge(sems["square_summed"], st.seen("square_summed"))
                    act(sq[:, k % 2, :], x_T[:, k, :], ACTF.Square).then_inc(sems["square_ready"], st.made("square_ready"))
                st.add("square_summed", 2)
                eng.wait_ge(sems["mean_ready"], st.seen("mean_ready"))
                act(rstd[:, :], rstd[:, :], ACTF.Sqrt).then_inc(sems["rstd_ready"], st.made("rstd_ready"))
                if final:
                    return
                for k in range(KT):
                    eng.wait_ge(sems["norm_tmp"], st.seen("norm_tmp"))
                    act(h_hi[:, k, :], ntmp[:, k % 2, :], ACTF.Copy).then_inc(sems["h_hi_ready"], st.made("h_hi_ready"))

            def proj(h):
                cols = slice(h * HALF, (h + 1) * HALF)

                def evac(g, dst, pieces=1, last=False, scale=1.0):
                    eng.wait_ge(sems["unit_done"], st.seen("unit_done"))
                    act(dst, bank(g), ACTF.Copy, scale=scale).then_inc(sems[f"{g}_free"], st.made(f"{g}_free"))
                    prep(pieces)

                for i in range(6):
                    evac("AB"[i % 2], cm[:, i, cols], 2 if i >= 6 else 1)
                evac("A", iq[:, 0, :], 2)
                evac("B", iq[:, 1, :], 2)
                evac("A", cm[:, 6, cols], 2, scale=DH ** -0.5)
                evac("B", cm[:, 7, cols], 1)
                eng.wait_ge(sems["unit_done"], st.seen("unit_done"))
                link(act(vw[:, TT * h:TT * (h + 1), :], bank("E").rearrange("p (t c) -> p t c", t=TT),
                            ACTF.Copy))
                eng.sem_inc(sems["E_free"], 1)
                eng.sem_inc(sems["cm_ready"], 1)
                prep()
                for n in range(2):
                    for j in range(4):
                        eng.wait_ge(sems["unit_done"], st.seen("unit_done"))
                        prep()
                    if n == 0:
                        for t, g in enumerate("CD"):
                            act(
                                r_in[:, 2 * t:2 * t + 2, 0:2, :].rearrange("p t a c -> p t (a c)"),
                                bank(g).rearrange("p (t c) -> p t c", t=2), ACTF.Copy).then_inc(sems[f"{g}_free"], st.made(f"{g}_free"))
                    else:
                        for t, g in enumerate("EFAB"):
                            link(act(r_in[:, t, 2:4, :].rearrange("p a c -> p (a c)"), bank(g), ACTF.Copy))
                            eng.sem_inc(sems[f"{g}_free"], 1)
                link(act(r_in[:, :, 3, :], r_in[:, :, 3, :], ACTF.Silu))
                eng.sem_inc(sems["ret_in"], 1)

            def scores(h):
                for b in range(max(2, TT * h), TT * (h + 1)):
                    for i in range(IDX_HEADS):
                        g = "CD"[i % 2]
                        eng.wait_ge(sems[f"{g}_to_act"], st.seen(f"{g}_to_act"))
                        eng.wait_ge(sems["relu_used"], st.taken("relu_used"))
                        act(relu[:, i % 2, 0:NK[b]], bank(g, 0, NK[b]), ACTF.Relu).then_inc(sems["relu_ready"], st.made("relu_ready"))
                eng.wait_ge(sems["relu_used"], st.now("relu_used"))

            def retention(h, l):
                eng.wait_ge(sems["A_to_act"], st.seen("A_to_act"))
                if h == 1:
                    load_s5(l)
                act(rqT[:, 0, :], bank("A"), ACTF.Copy).then_inc(sems["A_free"], st.made("A_free"))
                eng.wait_ge(sems["B_to_act"], st.seen("B_to_act"))
                act(rqT[:, 1, :], bank("B"), ACTF.Copy).then_inc(sems["B_free"], st.made("B_free"))
                eng.wait_ge(sems["C_to_act"], st.seen("C_to_act"))
                link(act(rkT[:, :, :], bank("C").rearrange("p (a c) -> p a c", a=2), ACTF.Copy))
                eng.sem_inc(sems["C_free"], 1)
                eng.sem_inc(sems["rT_ready"], 1)
                for c in range(TT):
                    eng.wait_ge(sems["D_to_act"], st.seen("D_to_act"))
                    out4 = r_in[:, c, 0, :].rearrange("p (a r e) -> p a r e", a=2, r=2)
                    for r in range(2):
                        ins = act(out4[:, :, r, :],
                                  bank("D", 512 * r, 512 * r + 128).rearrange("p (a e) -> p a e", a=2),
                                  ACTF.Copy)
                    link(ins)
                    eng.sem_inc(sems["D_free"], 1)
                eng.sem_inc(sems["o_ready"], 1)
                eng.wait_ge(sems["gvar_ready"], st.seen("gvar_ready"))
                act(gsum[:, 2, :], gsum[:, 2, :], ACTF.Sqrt).then_inc(sems["gstd_ready"], st.made("gstd_ready"))
                eng.wait_ge(sems["C_to_act"], st.seen("C_to_act"))
                link(act(ret_T[:, :, h * HALF:(h + 1) * HALF],
                            bank("C").rearrange("p (a c) -> p a c", a=2), ACTF.Copy))
                eng.sem_inc(sems["C_free"], 1)

            def load_s5(l):
                lay = ds(l, 1)

                def par(dst, src):
                    eng.dma_start(dst, src).then_inc(sems["s5_loaded"], st.made("s5_loaded", 16))

                for r in range(2):
                    half = slice(64 * r, 64 * r + 64)
                    par(s5_b[half, 0, :, :], b_re[lay, r::2, :, :].rearrange("l q n p -> n (l q) p"))
                    par(s5_b[half, 1, :, :], b_im[lay, r::2, :, :].rearrange("l q n p -> n (l q) p"))
                    par(s5_c[:, 0, :, 64 * r:64 * r + 64],
                        c_re[lay, :, :, :].rearrange("l (h g) p n -> (l g p) h n", h=2))
                    par(s5_c[:, 1, :, 64 * r:64 * r + 64],
                        c_im[lay, :, :, :].rearrange("l (h g) p n -> (l g p) h n", h=2))

            def s5():
                dt, adt, ang, cosarg = (s5p[:, i, :] for i in (3, 4, 5, 6))
                mag, mag8, sin1, cos1 = (s5p[:, i, :] for i in (7, 8, 9, 10))
                act(dt, s5p[:, 2, :], ACTF.Exp).then_inc(sems["dt_ready"], st.made("dt_ready"))
                eng.wait_ge(sems["angle_ready"], st.seen("angle_ready"))
                act(mag, adt, ACTF.Exp)
                act(mag8, adt, ACTF.Exp, scale=float(S5_STEPS))
                act(sin1, ang, ACTF.Sin)
                act(cos1, cosarg, ACTF.Sin).then_inc(sems["trig_ready"], st.made("trig_ready"))
                for hh in range(2):
                    for c, g in enumerate("CD"):
                        eng.wait_ge(sems[f"{g}_to_act"], st.seen(f"{g}_to_act"))
                        link(act(Vt[:, :, c, :], bank(g).rearrange("p (m s) -> p m s", m=8), ACTF.Copy))
                        eng.sem_inc(sems[f"{g}_free"], 1)
                    eng.sem_inc(sems["vt_ready"], 1)
                    for q, g in enumerate("ABCD"):
                        eng.wait_ge(sems[f"{g}_to_act"], st.seen(f"{g}_to_act"))
                        ins = act(Ht[:, :, q, :], bank(g, 0, 256).rearrange("p (c s) -> p c s", c=2),
                                  ACTF.Copy)
                        if q < 3:
                            ins.then_inc(sems[f"{g}_free"], st.made(f"{g}_free"))
                    link(ins)
                    eng.sem_inc(sems["D_free"], 1)
                    eng.sem_inc(sems["v_ready"], 1)
                    eng.wait_ge(sems["C_to_act"], st.seen("C_to_act"))
                    link(act(cm[:, hh, :].rearrange("p (c j) -> p j c", j=8),
                                bank("C").rearrange("p (j c) -> p j c", j=8), ACTF.Gelu_apprx_tanh))
                    eng.sem_inc(sems["C_free"], 1)
                    eng.sem_inc(sems["y_ready"], 1)
                for n in range(2):
                    for m in range(2):
                        g = "EFAB"[2 * n + m]
                        eng.wait_ge(sems[f"{g}_to_act"], st.seen(f"{g}_to_act"))
                        ins = act(Z2[:, m, n * HALF:(n + 1) * HALF], bank(g), ACTF.Sigmoid,
                                  bias=s5_col[:, 1, m:m + 1])
                        if 2 * n + m < 3:
                            ins.then_inc(sems[f"{g}_free"], st.made(f"{g}_free"))
                link(ins)
                eng.sem_inc(sems["B_free"], 1)
                eng.sem_inc(sems["sig_ready"], 1)

            Z2 = Z[:, :, :, :, :].rearrange("p a m q r -> p (a m q r)").rearrange("p (m t) -> p m t", m=2)

            def attend(h):
                for b in range(TT * h, TT * (h + 1)):
                    nk = NK[b]

                    def copies(i):
                        if b >= 4 or i % 2 == 0:
                            eng.wait_ge(sems["A_to_act"], st.seen("A_to_act"))
                            n = min(b + 1, 4) * P
                            act(probT[:, i % 2, 0:n], bank("A", 0, n), ACTF.Copy).then_inc(sems["ptA_ready"], st.made("ptA_ready"))

                    for i in range(HEADS):
                        g = "CD"[i % 2]
                        eng.wait_ge(sems["nmax_ready"], st.seen("nmax_ready"))
                        act(prob[:, i % 2, 0:nk], bank(g, 0, nk), ACTF.Exp,
                                                 bias=nmax[:, i:i + 1], accum_out=rsum[:, i:i + 1]).then_inc(sems["p_ready"], st.made("p_ready"))
                        if i >= 1:
                            copies(i - 1)
                    copies(HEADS - 1)
                    eng.wait_ge(sems["F_to_act"], st.seen("F_to_act"))
                    o = (b % TT) * P
                    act(h_hi[:, 2:6, o:o + P],
                                                  bank("F").rearrange("p (a c) -> p a c", a=4), ACTF.Copy).then_inc(sems["mix_hi_ready"], st.made("mix_hi_ready"))
                cols = slice(h * HALF, (h + 1) * HALF)
                if h == 0:
                    eng.wait_ge(sems["y_gated"], st.seen("y_gated"))
                act(h_hi[:, 0:2, :], cm[:, 0:2, cols], ACTF.Copy)
                act(h_hi[:, 6:8, :], ret_T[:, :, cols], ACTF.Copy).then_inc(sems["mix_hi_ready"], st.made("mix_hi_ready"))

            def mix_out():
                with st.loop(4, unit_done=2, hi_ready=2, raw_loaded0=16, raw_loaded1=16):
                    for e in range(2):
                        st.add("unit_done")
                        prep()

            def ffn(last):
                for c, n in enumerate(FF_CHUNKS):
                    with st.loop(n, unit_done=2, hi_ready=2, raw_loaded0=16, raw_loaded1=16,
                                 gate_used=1, gate_ready=1):
                        eng.wait_ge(sems["unit_done"], st.seen("unit_done"))
                        eng.wait_ge(sems["gate_used"], st.taken("gate_used"))
                        ins = act(gate[:, :], bank("A"), ACTF.Silu)
                        ins.then_inc(sems["gate_ready"], st.made("gate_ready"))
                        eng.wait_ge(sems["gate_ready"], st.value("gate_ready", st.count["gate_ready"]))
                        eng.sem_inc(sems["A_free"], 1)
                        prep()
                        st.add("unit_done")
                        prep()
                    tail = last and c == len(FF_CHUNKS) - 1
                    k = n // 2 - (1 if tail else 0)
                    with st.loop(k, unit_done=2, hi_ready=2, raw_loaded0=16, raw_loaded1=16):
                        for e in range(2):
                            st.add("unit_done")
                            prep()
                    if tail:
                        st.add("unit_done", 2)

            eng.wait_ge(sems["const_loaded"], 48)
            act(ident_b[:, :], ident, ACTF.Copy).then_inc(sems["ident_ready"], st.made("ident_ready"))
            eng.wait_ge(sems["E_to_act"], st.seen("E_to_act"))
            link(act(brow[:, :], bank("E", 0, 384)[0:HEADS, :], ACTF.Copy))
            eng.sem_inc(sems["E_free"], 1)
            eng.dma_start(
                bias_dram, brow[:, :].unsqueeze(1).broadcast_to([HEADS, P, 384])).then_inc(sems["bias_stored"], st.made("bias_stored", 16))
            eng.wait_ge(sems["bias_stored"], 16)
            eng.dma_start(
                bias_win[:, :, :],
                bass.AP(tensor=bias_dram.tensor, offset=P - 1, ap=[[383, P], [P * 384, HEADS], [1, 256]])).then_inc(sems["bias_loaded"], st.made("bias_loaded", 16))
            for t in range(NB):
                if t >= 2:
                    eng.wait_ge(sems["xtok_used"], st.seen("xtok_used"))
                eng.dma_start(xtok[:, t % 2, :], x[0, t * P:(t + 1) * P, :]).then_inc(sems[f"xtok_loaded{t % 2}"], st.made(f"xtok_loaded{t % 2}", 16))
                if t == 5:
                    eng.wait_ge(sems["x_updated"], st.seen("x_updated"))
                    store_x(0)
            st.add("xtok_used", 2)
            eng.wait_ge(sems["x_updated"], st.seen("x_updated"))
            store_x(1)
            with st.layers() as l:
                prep()
                prep()
                load_x(0)
                eng.wait_ge(sems["x_loaded"], st.value("x_loaded", st.count["x_loaded"]))
                eng.wait_ge(sems["params_loaded"], st.seen("params_loaded", 16 * 12))
                norm()
                proj(0)
                retention(0, l)
                scores(0)
                load_x(1)
                eng.wait_ge(sems["x_loaded"], st.value("x_loaded", st.count["x_loaded"]))
                norm()
                proj(1)
                load_x(0)
                retention(1, l)
                s5()
                scores(1)
                for h in range(2):
                    attend(h)
                    mix_out()
                    eng.wait_ge(sems["x_updated"], st.seen("x_updated"))
                    norm()
                    ffn(h == 1)
                    eng.wait_ge(sems["x_updated"], st.seen("x_updated"))
                    store_x(h)
                    if h == 0:
                        load_x(1)
                eng.sem_inc(sems["layer_done"], 1)
            for h in range(2):
                load_x(h)
                eng.wait_ge(sems["x_loaded"], st.value("x_loaded", st.count["x_loaded"]))
                norm(final=True)
                for t in range(TT):
                    eng.wait_ge(sems["fin_out"], st.seen("fin_out"))
                    ins = eng.dma_start(out[0, (h * TT + t) * P:(h * TT + t + 1) * P, :], xtok[:, t % 2, :])
                    ins.then_inc(sems[f"out_stored{t % 2}"], st.made(f"out_stored{t % 2}", 16))
            for e in range(2):
                eng.wait_ge(sems[f"out_stored{e}"], 16 * TT)

        @block.vector
        def _(eng):
            st = Counts(eng, "dve", sems["dve_held"])

            def link(ins):
                ins.then_inc(sems["dve_chain"], st.made("dve_chain"))
                eng.wait_ge(sems["dve_chain"], st.now("dve_chain"))

            def hold():
                eng.sem_inc(sems["dve_held"], 1)

            tt, ts, stt = eng.tensor_tensor, eng.tensor_scalar, eng.scalar_tensor_tensor
            MUL, ADD, SUB, MAX = ALU.mult, ALU.add, ALU.subtract, ALU.max

            def norm(which, final=False):
                gain = gain_last if final else gains[:, which, :]
                eng.wait_ge(sems["x_loaded"], st.seen("x_loaded", 16)) if which == 0 or final else None
                eng.wait_ge(sems["square_summed"], st.seen("square_summed", KT))
                link(ts(rstd[:, :], bank("F"), 1.0 / D, EPS, MUL, ADD))
                eng.sem_inc(sems["F_free"], 1)
                link(eng.reciprocal(rstd[:, :], rstd[:, :]))
                eng.sem_inc(sems["mean_ready"], 1)
                eng.wait_ge(sems["rstd_ready"], st.seen("rstd_ready"))
                if final:
                    for k in range(KT):
                        ins = stt(x_T[:, k, :], x_T[:, k, :], gain[:, k:k + 1], rstd[:, :], MUL, MUL)
                    link(ins)
                    eng.sem_inc(sems["fin_ready"], 1)
                    return

                def lo(k):
                    eng.wait_ge(sems["h_hi_ready"], st.seen("h_hi_ready"))
                    tt(h_lo[:, k, :], ntmp[:, k % 2, :], h_hi[:, k, :].bitcast(F32), SUB).then_inc(sems["h_ready"], st.made("h_ready"))

                for k in range(KT):
                    if k >= 2:
                        eng.wait_ge(sems["h_ready"], st.now("h_ready"))
                    stt(ntmp[:, k % 2, :], x_T[:, k, :], gain[:, k:k + 1],
                                              rstd[:, :], MUL, MUL).then_inc(sems["norm_tmp"], st.made("norm_tmp"))
                    if k >= 1:
                        lo(k - 1)
                lo(KT - 1)

            def scores(h):
                for b in range(max(2, TT * h), TT * (h + 1)):
                    s = score[b][:, :]
                    for i in range(IDX_HEADS):
                        g = "CD"[i % 2]
                        w = vw[:, b, 64 + i:65 + i]
                        r = relu[:, i % 2, 0:NK[b]]
                        eng.wait_ge(sems["relu_ready"], st.seen("relu_ready"))
                        if i == 0:
                            ins = ts(s, r, w, 0.0, MUL, ADD)
                        else:
                            ins = stt(s, r, w, s, MUL, ADD)
                        link(ins)
                        eng.sem_inc(sems[f"{g}_free"], 1)
                        eng.sem_inc(sems["relu_used"], 1)
                    last = score[b][:, NK[b] - P:NK[b]]
                    link(tt(last, last, table("noncausal"), ADD))

            def rounds(b, n):
                s = score[b][:, :]
                for _ in range(n):
                    hold()
                    link(eng.max(out=top8[:, :], in_=s))
                    hold()
                    link(eng.match_replace(out=s, in_to_replace=top8[:, :], in_values=s, imm_value=TAKEN))

            def mask(b):
                m = score[b][:, :].bitcast(BF16).rearrange("p (k two) -> p k two", two=2)[:, :, 0]
                link(ts(m, score[b][:, :], TAKEN, MASKED, ALU.not_equal, MUL))
                eng.sem_inc(sems["mask_ready"], 1)

            def topk_early():
                for b in (2, 3):
                    with st.loop(TOPK // 8, dve_chain=2):
                        rounds(b, 1)
                    mask(b)

            def some(b, n):
                with st.loop(n, dve_chain=2):
                    rounds(b, 1)

            def retention(h):
                eng.wait_ge(sems["ret_in"], st.seen("ret_in"))
                qk = r_in[:, :, 0:2, :].rearrange("p t a (h e) -> p t (a h) e", e=64)
                ro = rot[:, :, :, :].rearrange("p t a (h e) -> p t (a h) e", e=64)
                x1, x2 = qk[:, :, :, 0:32], qk[:, :, :, 32:64]
                o1, o2 = ro[:, :, :, 0:32], ro[:, :, :, 32:64]
                shape = [P, TT, 8, 32]

                def trig(name):
                    t = table(name).rearrange("p (t e) -> p t e", e=32)[:, TT * h:TT * (h + 1), :]
                    return t.unsqueeze(2).broadcast_to(shape)

                ta = rtmp[:, 0, :].rearrange("p (t a e) -> p t a e", t=TT, a=8)
                tb = rtmp[:, 1, :].rearrange("p (t a e) -> p t a e", t=TT, a=8)
                tt(ta, x1, trig("cos"), MUL)
                link(tt(tb, x2, trig("sin"), MUL))
                link(tt(o1, ta, tb, SUB))
                tt(ta, x2, trig("cos"), MUL)
                link(tt(tb, x1, trig("sin"), MUL))
                link(tt(o2, ta, tb, ADD))
                eng.sem_inc(sems["rot_ready"], 1)
                kw = r_in[:, :, 1, :].rearrange("p t (h e) -> p t h e", e=64)
                rk = rot[:, :, 1, :].rearrange("p t (h e) -> p t h e", e=64)
                wk = table("wk").unsqueeze(1).unsqueeze(3).broadcast_to([P, TT, RH, 64])
                tt(kw, rk, wk, MUL)
                eng.wait_ge(sems["rT_ready"], st.seen("rT_ready"))
                qs = rtmp[:, 0, :].rearrange("p (a c i) -> p a c i", a=2, c=TT)
                rq = rqT[:, :, :].rearrange("p a (c i) -> p a c i", c=TT)
                wq = table("wq").rearrange("p (a i) -> p a i", a=2).unsqueeze(2).broadcast_to([P, 2, TT, P])
                link(tt(qs, rq, wq, MUL))
                if h == 0:
                    link(eng.memset(state[:, 0, :, :], 0.0))
                eng.sem_inc(sems["qs_ready"], 1)
                dec = table("decay").rearrange("p (a r i) -> p a r i", a=2, r=2)
                for c in range(TT):
                    inner = rtmp[:, 1, (c % 2) * 512:(c % 2) * 512 + 512].rearrange(
                        "p (a r i) -> p a r i", a=2, r=2)
                    for r, g in enumerate("EF"):
                        eng.wait_ge(sems[f"{g}_to_dve"], st.seen(f"{g}_to_dve"))
                        link(tt(inner[:, :, r, :], bank(g, 0, 256).rearrange("p (a i) -> p a i", a=2),
                                   dec[:, :, r, :], MUL))
                        eng.sem_inc(sems[f"{g}_free"], 1)
                    eng.sem_inc(sems["st_ready"], 1)
                    eng.wait_ge(sems["A_to_dve"], st.seen("A_to_dve"))
                    for a in range(2):
                        o, _ = at["gchunk"]
                        ins = stt(state[:, (c + 1) % 2, a, :], state[:, c % 2, a, :], cst[:, o + a:o + a + 1],
                                  bank("A", a * 64, a * 64 + 64), MUL, ADD)
                    link(ins)
                    eng.sem_inc(sems["A_free"], 1)
                    eng.sem_inc(sems["state_ready"], 1)
                eng.wait_ge(sems["o_ready"], st.seen("o_ready"))
                o = r_in[:, :, 0, :].rearrange("p t (h e) -> p t h e", e=64)
                sqr = rot[:, :, 0, :].rearrange("p t (h e) -> p t h e", e=64)

                def stat(i):
                    return gsum[:, i, :].rearrange("p (t h) -> p t h", t=TT)

                def spread(i):
                    return stat(i).unsqueeze(3).broadcast_to([P, TT, RH, 64])

                link(eng.tensor_reduce(stat(0), o, AX_X, ADD))
                link(ts(gsum[:, 1, :], gsum[:, 0, :], 1.0 / 64, None, MUL))
                link(tt(o, o, spread(1), SUB))
                link(tt(sqr, o, o, MUL))
                link(eng.tensor_reduce(stat(3), sqr, AX_X, ADD))
                link(ts(gsum[:, 3, :], gsum[:, 3, :], 1.0 / 64, EPS, MUL, ADD))
                link(eng.reciprocal(gsum[:, 2, :], gsum[:, 3, :]))
                eng.sem_inc(sems["gvar_ready"], 1)
                eng.wait_ge(sems["gstd_ready"], st.seen("gstd_ready"))
                link(tt(o, o, spread(2), MUL))
                flat = r_in[:, :, 0, :]
                link(tt(flat, flat, gn_row[:, :].unsqueeze(1).broadcast_to([P, TT, 256]), MUL))
                link(tt(flat, flat, r_in[:, :, 3, :], MUL))
                eng.sem_inc(sems["ret_out"], 1)

            def s5():
                s = [s5p[:, i, :] for i in range(64)]
                ar, ai, _, dt, adt, ang, cosarg, mag, mag8, sin1, cos1 = s[:11]
                t1, t2, t3, t4, cr, ci, den = s[11:18]
                PR, PI = 20, 30
                RR, RI = 40, 48

                def cmul(orr, oi, xr, xi, yr, yi, a, b, c, d):
                    tt(a, xr, yr, MUL)
                    tt(b, xi, yi, MUL)
                    tt(c, xr, yi, MUL)
                    link(tt(d, xi, yr, MUL))
                    tt(orr, a, b, SUB)
                    link(tt(oi, c, d, ADD))

                eng.wait_ge(sems["s5_loaded"], st.seen("s5_loaded", 16 * 8))
                eng.wait_ge(sems["dt_ready"], st.seen("dt_ready"))
                tt(adt, ar, dt, MUL)
                link(tt(t1, ai, dt, MUL))
                magic = 12582912.0
                link(ts(t2, t1, 1.0 / (2 * np.pi), magic, MUL, ADD))
                link(ts(t2, t2, magic, None, SUB))
                for part in (6.28125, 0.0019350051879882812, 3.0199159819567e-07):
                    link(stt(t1, t2, -part, t1, MUL, ADD))
                link(ts(ang, t1, 3.1415925, -3.1415925, ALU.min, MAX))
                link(ts(t3, ang, -1.0, None, MUL))
                link(tt(t3, ang, t3, MAX))
                link(ts(cosarg, t3, -1.0, float(np.pi / 2), MUL, ADD))
                eng.sem_inc(sems["angle_ready"], 1)
                link(eng.memset(s5_ct[:, :, :, :], 0.0))
                for lo in (0, 4):
                    link(eng.memset(Z[:, lo // 4, :, :, :], 0.0))
                eng.wait_ge(sems["trig_ready"], st.seen("trig_ready"))
                tt(s[PR + 1], mag, cos1, MUL)
                tt(s[PI + 1], mag, sin1, MUL)
                eng.memset(s[PR], 1.0)
                eng.memset(s[PI], 0.0)
                tt(t1, ar, ar, MUL)
                link(tt(t2, ai, ai, MUL))
                link(tt(den, t1, t2, ADD))
                link(eng.reciprocal(den, den))
                link(ts(s[18], s[PR + 1], 1.0, None, SUB))
                tt(t1, s[18], ar, MUL)
                tt(t2, s[PI + 1], ai, MUL)
                tt(t3, s[PI + 1], ar, MUL)
                link(tt(t4, s[18], ai, MUL))
                tt(cr, t1, t2, ADD)
                link(tt(ci, t3, t4, SUB))
                tt(cr, cr, den, MUL)
                link(tt(ci, ci, den, MUL))
                cmul(s[PR + 2], s[PI + 2], s[PR + 1], s[PI + 1], s[PR + 1], s[PI + 1], t1, t2, t3, t4)
                for k, n in ((2, 2), (4, 4)):
                    for j in range(n):
                        cmul(s[PR + k + 1 + j], s[PI + k + 1 + j], s[PR + 1 + j], s[PI + 1 + j],
                             s[PR + k], s[PI + k], t1, t2, t3, t4)
                tt(s[RR], cos1, cos1, MUL)
                cmul(s[RR], s[RI], cos1, sin1, cos1, sin1, t1, t2, t3, t4)
                cmul(s[RR + 1], s[RI + 1], s[RR], s[RI], s[RR], s[RI], t1, t2, t3, t4)
                cmul(s[RR], s[RI], s[RR + 1], s[RI + 1], s[RR + 1], s[RI + 1], t1, t2, t3, t4)
                for k in range(6):
                    cmul(s[RR + k + 1], s[RI + k + 1], s[RR + k], s[RI + k], s[RR + k], s[RI + k],
                         t1, t2, t3, t4)
                crb, cib = (a.unsqueeze(2).broadcast_to([P, 8, 16]) for a in (cr, ci))
                br, bi = s5_b[:, 0, :, :], s5_b[:, 1, :, :]
                tt(s5_t[:, 0, :, :], crb, br, MUL)
                link(tt(s5_t[:, 1, :, :], cib, bi, MUL))
                link(tt(s5_bb[:, 0, :, :], s5_t[:, 0, :, :], s5_t[:, 1, :, :], SUB))
                tt(s5_t[:, 0, :, :], crb, bi, MUL)
                link(tt(s5_t[:, 1, :, :], cib, br, MUL))
                link(tt(s5_bb[:, 1, :, :], s5_t[:, 0, :, :], s5_t[:, 1, :, :], ADD))
                eng.wait_ge(sems["E_to_dve"], st.seen("E_to_dve"))
                for r in range(2):
                    rows_ = slice(64 * r, 64 * r + 64)
                    src = bank("E").rearrange("p (c q r e) -> p c q r e", c=2, r=2, e=16)
                    for c, sign in ((0, 1.0), (1, -1.0)):
                        ins = ts(s5_ct[rows_, c, :, 16 * r:16 * r + 16], src[rows_, c, :, r, :], sign, None, MUL)
                link(ins)
                eng.sem_inc(sems["E_free"], 1)
                pw = [s5p[:, o:o + 9, :] for o in (PR, PI)]
                xa, xb = Xt[:, 0, :], Xt[:, 1, :]
                for hh in range(2):
                    if hh == 1:
                        eng.wait_ge(sems["y_ready"], st.seen("y_ready"))
                    qs = slice(4 * hh, 4 * hh + 4)
                    zs = [P, 8, 4, 16]
                    za, zb = (t.rearrange("p (m q e) -> p m q e", m=8, q=4) for t in (xa, xb))

                    def power(c, sl=slice(0, 8), shape=zs):
                        return pw[c][:, sl, qs].unsqueeze(3).broadcast_to(shape)

                    def inp(c):
                        return s5_bb[:, c, qs, :].unsqueeze(1).broadcast_to(zs)

                    for c in range(2):
                        tt(za, power(0), inp(c), MUL)
                        link(tt(zb, power(1), inp(1 - c), MUL))
                        for r in range(2):
                            rows_ = slice(64 * r, 64 * r + 64)
                            ins = tt(Z[rows_, c, :, :, 16 * r:16 * r + 16], za[rows_], zb[rows_],
                                     ADD if c else SUB)
                        link(ins)
                    eng.sem_inc(sems["z_ready"], 1)
                    ys = [P, 4, 4, 32]
                    ya, yb = (t.rearrange("p (m q e) -> p m q e", m=4, q=4) for t in (xa, xb))
                    for m in range(2):
                        sl = slice(1 + 4 * m, 5 + 4 * m)
                        cr_, ni_ = (s5_ct[:, c, qs, :].unsqueeze(1).broadcast_to(ys) for c in range(2))
                        tt(ya, power(0, sl, ys), cr_, MUL)
                        link(tt(yb, power(1, sl, ys), ni_, MUL))
                        flat = [Yt[:, c, 4 * m:4 * m + 4, :, :].rearrange("p m q e -> p (m q e)")
                                for c in range(2)]
                        link(tt(flat[0], xa, xb, ADD))
                        tt(ya, power(1, sl, ys), cr_, MUL)
                        link(tt(yb, power(0, sl, ys), ni_, MUL))
                        link(tt(flat[1], xb, xa, SUB))
                    for a, g in enumerate("EF"):
                        eng.wait_ge(sems[f"{g}_to_dve"], st.seen(f"{g}_to_dve"))
                        link(tt(Kt[:, 4 * a:4 * a + 4, :], bank(g).rearrange("p (m o) -> p m o", m=4),
                                   table("quads").unsqueeze(1).broadcast_to([P, 4, P]), MUL))
                        eng.sem_inc(sems[f"{g}_free"], 1)
                    link(stt(Kt[:, 0, :], ident, s5_col[:, 0, hh:hh + 1], Kt[:, 0, :], MUL, ADD))
                    eng.sem_inc(sems["kt_ready"], 1)
                    eng.memset(Et[:, 0, :, 0:1], 1.0)
                    link(eng.memset(Et[:, 1, :, 0:1], 0.0))
                    for k in range(7):
                        n = 1 << k
                        sh = [P, 4, n]
                        rr, ri = (s5p[:, o + k, qs].unsqueeze(2).broadcast_to(sh) for o in (RR, RI))
                        tmp = [Xt[:, i // 2, (i % 2) * 256:(i % 2) * 256 + 4 * n].rearrange(
                            "p (q c) -> p q c", q=4) for i in range(4)]
                        cmul(Et[:, 0, :, n:2 * n], Et[:, 1, :, n:2 * n], Et[:, 0, :, 0:n], Et[:, 1, :, 0:n],
                             rr, ri, *tmp)
                    def flat4(t, c):
                        return t[:, c, :, :].rearrange("p q c -> p (q c)")

                    er, ei = flat4(Et, 0), flat4(Et, 1)
                    eng.wait_ge(sems["v_ready"], st.seen("v_ready"))
                    hr, hi = flat4(Ht, 0), flat4(Ht, 1)
                    gr, gi = flat4(Gt, 0), flat4(Gt, 1)
                    tt(xa, er, hr, MUL)
                    link(tt(xb, ei, hi, MUL))
                    link(tt(gr, xa, xb, ADD))
                    tt(xa, er, hi, MUL)
                    link(tt(xb, ei, hr, MUL))
                    link(tt(gi, xa, xb, SUB))
                    for c in range(2):
                        for q in range(4):
                            decay = mag8[:, 4 * hh + q:4 * hh + q + 1].broadcast_to([P, P])
                            ins = eng.tensor_tensor_scan(Ht[:, c, q, :], decay, Gt[:, c, q, :], 0.0,
                                                         op0=MUL, op1=ADD)
                    link(ins)
                    tt(xa, er, hr, MUL)
                    link(tt(xb, ei, hi, MUL))
                    x4 = [t.rearrange("p (q c) -> p q c", q=4)[:, :, 0:P - 1] for t in (xa, xb)]
                    eng.memset(Gt[:, 0, :, 0:1], 0.0)
                    eng.memset(Gt[:, 1, :, 0:1], 0.0)
                    link(tt(Gt[:, 0, :, 1:P], x4[0], x4[1], SUB))
                    tt(xa, er, hi, MUL)
                    link(tt(xb, ei, hr, MUL))
                    link(tt(Gt[:, 1, :, 1:P], x4[0], x4[1], ADD))
                    eng.sem_inc(sems["hprev_ready"], 1)
                eng.wait_ge(sems["sig_ready"], st.seen("sig_ready"))
                z2 = Z[:, :, :, :, :].rearrange("p a m q r -> p (a m q r)").rearrange("p (m t) -> p m t", m=2)
                link(tt(cm[:, 0:2, :], cm[:, 0:2, :], z2, MUL))
                eng.sem_inc(sems["y_gated"], 1)

            def attend(h):
                for b in range(TT * h, TT * (h + 1)):
                    nk = NK[b]
                    win = min(256, nk)

                    def copies(i):
                        if b >= 4 or i % 2 == 1:
                            eng.wait_ge(sems["B_to_dve"], st.seen("B_to_dve"))
                            lo, n = (512, nk - 512) if b >= 4 else (0, nk)
                            eng.tensor_copy(probT[:, i % 2, lo:lo + n],
                                                                   bank("B", 0, n)).then_inc(sems["ptB_ready"], st.made("ptB_ready"))

                    for i in range(HEADS):
                        g = "CD"[i % 2]
                        eng.wait_ge(sems[f"{g}_to_dve"], st.seen(f"{g}_to_dve"))
                        near = bank(g, nk - win, nk)
                        link(tt(near, near, bias_win[:, i, 256 - win:256], ADD))
                        eng.tensor_reduce(nmax[:, i:i + 1], bank(g, 0, nk), AX_X,
                                                                  MAX, negate=True).then_inc(sems["nmax_ready"], st.made("nmax_ready"))
                        if i >= 1:
                            copies(i - 1)
                    copies(HEADS - 1)
                    eng.wait_ge(sems["E_to_dve"], st.seen("E_to_dve"))
                    link(eng.reciprocal(rinv[:, :], rsum[:, :]))
                    link(tt(ao[:, :].rearrange("p (h e) -> p h e", h=HEADS),
                               bank("E").rearrange("p (h e) -> p h e", h=HEADS),
                               rinv[:, :].unsqueeze(2).broadcast_to([P, HEADS, DH]), MUL))
                    eng.sem_inc(sems["E_free"], 1)
                    eng.sem_inc(sems["ao_ready"], 1)
                    eng.wait_ge(sems["mix_hi_ready"], st.seen("mix_hi_ready"))
                    o = (b % TT) * P
                    link(tt(h_lo[:, 2:6, o:o + P], bank("F").rearrange("p (a c) -> p a c", a=4),
                               h_hi[:, 2:6, o:o + P].bitcast(F32), SUB))
                    eng.sem_inc(sems["F_free"], 1)
                    eng.sem_inc(sems["mix_ready"], 1)
                eng.wait_ge(sems["mix_hi_ready"], st.seen("mix_hi_ready"))
                cols = slice(h * HALF, (h + 1) * HALF)
                tt(h_lo[:, 0:2, :], cm[:, 0:2, cols], h_hi[:, 0:2, :].bitcast(F32), SUB)
                tt(h_lo[:, 6:8, :], ret_T[:, :, cols], h_hi[:, 6:8, :].bitcast(F32), SUB).then_inc(sems["mix_ready"], st.made("mix_ready"))

            def mix_out(h):
                if h == 0:
                    st.add("unit_done", 2 * UNITS_PROJ)
                eng.wait_ge(sems["x_loaded"], st.seen("x_loaded", 16))
                with st.loop(4, unit_done=2, dve_chain=2) as i:
                    for e, g in enumerate("AB"):
                        eng.wait_ge(sems["unit_done"], st.seen("unit_done"))
                        xk = x_T[:, ds(i * 2 + e, 1), :].rearrange("p o c -> p (o c)")
                        link(tt(xk, xk, bank(g), ADD))
                        eng.sem_inc(sems[f"{g}_free"], 1)
                eng.sem_inc(sems["x_updated"], 1)

            def ffn(early=None):
                for c, n in enumerate(FF_CHUNKS):
                    step, after = early[c] if early else ((), ())
                    chain = 2 + 2 * sum(k for _, k in step)
                    with st.loop(n, unit_done=2, gate_ready=1, dve_chain=chain, a_ready=1) as i:
                        st.add("unit_done")
                        eng.wait_ge(sems["gate_ready"], st.seen("gate_ready"))
                        eng.wait_ge(sems["unit_done"], st.seen("unit_done"))
                        link(tt(atmp[:, :], bank("B"), gate[:, :], MUL))
                        eng.sem_inc(sems["B_free"], 1)
                        eng.sem_inc(sems["gate_used"], 1)
                        hi = a_hi[:, ds(i, 1), :].rearrange("p o c -> p (o c)")
                        lo = a_lo[:, ds(i, 1), :].rearrange("p o c -> p (o c)")
                        link(eng.tensor_copy(hi, atmp[:, :]))
                        tt(lo, atmp[:, :], hi.bitcast(F32), SUB).then_inc(sems["a_ready"], st.made("a_ready"))
                        eng.wait_ge(sems["a_ready"], st.now("a_ready"))
                        for b, k in step:
                            rounds(b, k)
                    for b, k in after:
                        some(b, k)
                    eng.wait_ge(sems["unit_done"], st.seen("unit_done", n))
                    for g, (first, k) in GROUPS.items():
                        xk = x_T[:, first:first + k, :].rearrange("p k c -> p (k c)")
                        link(tt(xk, xk, bank(g), ADD))
                        eng.sem_inc(sems[f"{g}_free"], 1)
                eng.sem_inc(sems["x_updated"], 1)

            eng.wait_ge(sems["const_loaded"], 48)
            ts(causal_b[:, :], table("noncausal"), MASKED / NONCAUSAL, None, MUL).then_inc(sems["ident_ready"], st.made("ident_ready"))
            for t in range(NB):
                g = "CD"[t % 2]
                if t == TT:
                    eng.wait_ge(sems["x_stored"], st.seen("x_stored", 16))
                eng.wait_ge(sems[f"{g}_to_dve"], st.seen(f"{g}_to_dve"))
                c = (t % TT) * P
                link(eng.tensor_copy(x_T[:, :, c:c + P], bank(g).rearrange("p (k c) -> p k c", k=KT)))
                eng.sem_inc(sems[f"{g}_free"], 1)
                eng.sem_inc(sems["xtok_used"], 1)
                if t % TT == TT - 1:
                    eng.sem_inc(sems["x_updated"], 1)
            with st.layers():
                norm(0)
                retention(0)
                scores(0)
                norm(0)
                topk_early()
                retention(1)
                s5()
                scores(1)
                attend(0)
                mix_out(0)
                norm(1)
                ffn([(((4, 4),), ((5, 22),)), (((6, 4),), ((5, 10), (7, 8))), (((7, 3),), ((7, 6),))])
                for b in range(4, NB):
                    mask(b)
                attend(1)
                mix_out(1)
                norm(1)
                ffn()
            for h in range(2):
                norm(0, final=True)
                for t in range(TT):
                    g = "CD"[t % 2]
                    eng.wait_ge(sems[f"{g}_to_dve"], st.seen(f"{g}_to_dve"))
                    if h * TT + t >= 2:
                        eng.wait_ge(sems[f"out_stored{t % 2}"], st.seen(f"out_stored{t % 2}", 16))
                    link(eng.tensor_copy(xtok[:, t % 2, :], bank(g)))
                    eng.sem_inc(sems[f"{g}_free"], 1)
                    eng.sem_inc(sems["fin_out"], 1)

        @block.tensor
        def _(eng):
            st = Counts(eng, "pe", sems["pe_held"])

            def mm(out_, lhsT, rhs, start, stop):
                return eng.matmul(out_, lhsT, rhs, start=start, stop=stop, skip_group_check=True)

            def take(*groups):
                for g in groups:
                    eng.wait_ge(sems[f"{g}_free"], st.taken(f"{g}_free"))

            def give(g, to, ins):
                ins.then_inc(sems[f"{g}_to_{to}"], st.made(f"{g}_to_{to}"))

            PARTS = ((w_hi, 0), (w_hi, 1), (w_lo, 0))

            def norm():
                take("F")
                for k in range(KT):
                    eng.wait_ge(sems["square_ready"], st.seen("square_ready"))
                    mm(bank("F"), table("ones"), sq[:, k % 2, :], k == 0, k == KT - 1).then_inc(sems["square_summed"], st.made("square_summed"))

            def unit(g):
                slot = st.count.get("weights_ready", 0) % 2
                eng.wait_ge(sems["weights_ready"], st.seen("weights_ready"))
                take(g)
                for k in range(KT):
                    for j, (w, part) in enumerate(PARTS):
                        ins = mm(bank(g), w[:, slot, k * P:(k + 1) * P], (h_hi, h_lo)[part][:, k, :],
                                 k == 0 and j == 0, k == KT - 1 and j == 2)
                ins.then_inc(sems["unit_done"], st.made("unit_done"))

            def units(times):
                with st.loop(times, weights_ready=2, unit_done=2, A_free=1, B_free=1):
                    unit("A")
                    unit("B")

            def token_mms(out_, t, k, w, start, stop):
                cols = slice(t * P, (t + 1) * P)
                parts = ((h_hi, 0), (h_hi, 1), (h_lo, 0))
                for j, (x_, part) in enumerate(parts):
                    ins = mm(out_, x_[:, k, cols], w[part], start and j == 0, stop and j == 2)
                return ins

            def proj():
                eng.wait_ge(sems["h_ready"], st.seen("h_ready", KT))
                units(5)
                slot = st.count["weights_ready"] % 2
                eng.wait_ge(sems["weights_ready"], st.seen("weights_ready"))
                take("E")
                for t in range(TT):
                    for k in range(KT):
                        w = [x_[:, slot, k * P:(k + 1) * P] for x_ in (w_hi, w_lo)]
                        ins = token_mms(bank("E", t * P, (t + 1) * P), t, k, w, k == 0, k == KT - 1)
                ins.then_inc(sems["unit_done"], st.made("unit_done"))
                for n in range(2):
                    if n == 0:
                        take("C", "D")
                        outs = [bank("C", 0, 512), bank("C", 512, 1024), bank("D", 0, 512), bank("D", 512, 1024)]
                    else:
                        take("E", "F", "A", "B")
                        outs = [bank(g) for g in "EFAB"]
                    for j in range(4):
                        slot = st.count["weights_ready"] % 2
                        eng.wait_ge(sems["weights_ready"], st.seen("weights_ready"))
                        for t in range(TT):
                            for k in range(2):
                                w = [x_[:, slot, k * 512:(k + 1) * 512] for x_ in (w_hi, w_lo)]
                                ins = token_mms(outs[t], t, 2 * j + k, w, j == 0 and k == 0,
                                                j == 3 and k == 1)
                        ins.then_inc(sems["unit_done"], st.made("unit_done"))

            def scores(h):
                if h == 0:
                    eng.wait_ge(sems["cm_ready"], st.seen("cm_ready"))
                else:
                    eng.wait_ge(sems["cm_ready"], st.seen("cm_ready"))
                for b in range(max(2, TT * h), TT * (h + 1)):
                    q = slice((b % TT) * P, (b % TT + 1) * P)
                    for i in range(IDX_HEADS):
                        g = "CD"[i % 2]
                        r = slice(64 * (i % 2), 64 * (i % 2) + 64)
                        take(g)
                        for a in range(0, NK[b], 512):
                            n = min(512, NK[b] - a)
                            ins = mm(bank(g, a, a + n), iq[r, i // 2, q], cm[r, 7, a:a + n], True, True)
                        give(g, "act", ins)

            def retention(h):
                eng.wait_ge(sems["rot_ready"], st.seen("rot_ready"))
                take("A", "B", "C")
                for a in range(2):
                    for t in range(TT):
                        ins = eng.transpose(bank("AB"[a], t * P, (t + 1) * P),
                                            rot[:, t, 0, a * P:(a + 1) * P], ident)
                    give("AB"[a], "act", ins)
                for a in range(2):
                    for t in range(TT):
                        ins = eng.transpose(bank("C", a * 512 + t * P, a * 512 + (t + 1) * P),
                                            rot[:, t, 1, a * P:(a + 1) * P], ident)
                give("C", "act", ins)
                eng.wait_ge(sems["qs_ready"], st.seen("qs_ready"))
                qs = rtmp[:, 0, :].rearrange("p (a c i) -> p a c i", a=2, c=TT)
                for c in range(TT):
                    cols = slice(c * P, (c + 1) * P)
                    for r, g in enumerate("EF"):
                        half = slice(64 * r, 64 * r + 64)
                        take(g)
                        for a in range(2):
                            ins = mm(bank(g, a * P, (a + 1) * P), rkT[half, a, cols], rqT[half, a, cols],
                                     True, True)
                        give(g, "dve", ins)
                    inner = rtmp[:, 1, (c % 2) * 512:(c % 2) * 512 + 512].rearrange(
                        "p (a r i) -> p a r i", a=2, r=2)
                    eng.wait_ge(sems["st_ready"], st.seen("st_ready"))
                    if c:
                        eng.wait_ge(sems["state_ready"], st.seen("state_ready"))
                    take("D")
                    for r in range(2):
                        half = slice(64 * r, 64 * r + 64)
                        for a in range(2):
                            hd = 2 * a + r
                            o = bank("D", 512 * r + a * 64, 512 * r + a * 64 + 64)
                            mm(o, inner[:, a, r, :], r_in[:, c, 2, 64 * hd:64 * hd + 64], True, False)
                            ins = mm(o, qs[half, a, c, :], state[half, c % 2, a, :], False, True)
                    give("D", "act", ins)
                    take("A")
                    for r in range(2):
                        for a in range(2):
                            hd = 2 * a + r
                            ins = mm(bank("A", a * 64, a * 64 + 64)[64 * r:64 * r + 64, :],
                                     r_in[:, c, 1, 64 * hd:64 * hd + 64],
                                     r_in[:, c, 2, 64 * hd:64 * hd + 64], True, True)
                    give("A", "dve", ins)
                eng.wait_ge(sems["state_ready"], st.seen("state_ready"))
                eng.wait_ge(sems["ret_out"], st.seen("ret_out"))
                take("C")
                for a in range(2):
                    for t in range(TT):
                        ins = eng.transpose(bank("C", a * 512 + t * P, a * 512 + (t + 1) * P),
                                            r_in[:, t, 0, a * P:(a + 1) * P], ident)
                give("C", "act", ins)

            def s5():
                take("E")
                eng.wait_ge(sems["s5_loaded"], st.seen("s5_loaded", 16 * 8))
                for c in range(2):
                    for hh in range(2):
                        o = (2 * c + hh) * P
                        ins = eng.transpose(bank("E", o, o + P), s5_c[:, c, hh, :], ident)
                give("E", "dve", ins)
                for hh in range(2):
                    u = cm[:, hh, :].rearrange("p (c j) -> p j c", j=8)
                    eng.wait_ge(sems["z_ready"], st.seen("z_ready"))
                    for c, g in enumerate("CD"):
                        take(g)
                        for m in range(8):
                            ins = eng.transpose(bank(g, m * P, (m + 1) * P),
                                                Z[:, c, m, :, :].rearrange("p q e -> p (q e)"), ident)
                        give(g, "act", ins)
                    for a, g in enumerate("EF"):
                        take(g)
                        for m in range(4 * a, 4 * a + 4):
                            o = (m % 4) * P
                            for c in range(2):
                                ins = mm(bank(g, o, o + P), Z[:, c, m, :, :].rearrange("p q e -> p (q e)"),
                                         s5_ct[:, c, 4 * hh:4 * hh + 4, :].rearrange("p q e -> p (q e)"),
                                         c == 0, c == 1)
                        give(g, "dve", ins)
                    eng.wait_ge(sems["vt_ready"], st.seen("vt_ready"))
                    for q, g in enumerate("ABCD"):
                        take(g)
                        rows_ = slice(32 * q, 32 * q + 32)
                        for c in range(2):
                            for j in range(8):
                                ins = mm(bank(g, c * P, (c + 1) * P), Vt[rows_, 7 - j, c, :], u[rows_, j, :],
                                         j == 0, j == 7)
                        give(g, "act", ins)
                    eng.wait_ge(sems["kt_ready"], st.seen("kt_ready"))
                    eng.wait_ge(sems["hprev_ready"], st.seen("hprev_ready"))
                    take("C")
                    for j in range(8):
                        o = bank("C", j * P, (j + 1) * P)
                        for i in range(j + 1):
                            mm(o, Kt[:, j - i, :], u[:, i, :], i == 0, False)
                        for q in range(4):
                            for c in range(2):
                                ins = mm(o[32 * q:32 * q + 32, :], Yt[:, c, j, q, :], Gt[:, c, q, :], False, c == 1)
                    give("C", "act", ins)
                eng.wait_ge(sems["y_ready"], st.seen("y_ready", 2))
                for n in range(2):
                    for m in range(2):
                        g = "EFAB"[2 * n + m]
                        take(g)
                        for k in range(2):
                            ins = mm(bank(g), s5_glu[:, k, m * P:(m + 1) * P],
                                     cm[:, k, n * HALF:(n + 1) * HALF], k == 0, k == 1)
                        give(g, "act", ins)

            def attend(h):
                masks = range(2, 4) if h == 0 else range(4, NB)
                eng.wait_ge(sems["mask_ready"], st.seen("mask_ready", len(masks)))
                for b in range(TT * h, TT * (h + 1)):
                    nk, q = NK[b], slice(b * P, (b + 1) * P)
                    if b >= 2:
                        m = score[b][:, :].bitcast(BF16).rearrange("p (k two) -> p k two", two=2)[:, :, 0]

                    def logits(i):
                        g = "CD"[i % 2]
                        r = slice(64 * (i % 2), 64 * (i % 2) + 64)
                        take(g)
                        for a in range(0, nk, 512):
                            n = min(512, nk - a)
                            mm(bank(g, a, a + n), cm[r, CM_Q + i // 2, q], cm[r, 6, a:a + n], True, False)
                            if b >= 2:
                                ins = mm(bank(g, a, a + n), ident_b[:, :], m[:, a:a + n], False, True)
                            else:
                                ins = mm(bank(g, nk - P, nk), ident_b[:, :], causal_b[:, :], False, True)
                        give(g, "dve", ins)

                    def turn(i):
                        eng.wait_ge(sems["p_ready"], st.seen("p_ready"))
                        eng.sem_inc(sems["CD"[i % 2] + "_free"], 1)
                        if i:
                            turned(i - 1)
                        if b >= 4:
                            parts = (("A", 0, 4, "act"), ("B", 4, b + 1, "dve"))
                        else:
                            parts = ((("A", 0, b + 1, "act"), ("B", 0, b + 1, "dve"))[i % 2],)
                        for g, k0, k1, to in parts:
                            take(g)
                            for k in range(k0, k1):
                                ins = eng.transpose(bank(g, (k - k0) * P, (k - k0 + 1) * P),
                                                    prob[:, i % 2, k * P:(k + 1) * P], ident)
                            give(g, to, ins)

                    def turned(i):
                        if b >= 4 or i % 2 == 0:
                            eng.wait_ge(sems["ptA_ready"], st.seen("ptA_ready"))
                            eng.sem_inc(sems["A_free"], 1)
                        if b >= 4 or i % 2 == 1:
                            eng.wait_ge(sems["ptB_ready"], st.seen("ptB_ready"))
                            eng.sem_inc(sems["B_free"], 1)

                    def values(i):
                        for k in range(b + 1):
                            ins = mm(bank("E", i * DH, (i + 1) * DH), probT[:, i % 2, k * P:(k + 1) * P],
                                     vw[:, k, 0:DH], k == 0, k == b)
                        return ins

                    take("E")
                    logits(0)
                    logits(1)
                    for i in range(HEADS):
                        turn(i)
                        if i + 2 < HEADS:
                            logits(i + 2)
                        if i >= 1:
                            values(i - 1)
                    turned(HEADS - 1)
                    give("E", "dve", values(HEADS - 1))
                    eng.wait_ge(sems["ao_ready"], st.seen("ao_ready"))
                    take("F")
                    for a in range(4):
                        ins = eng.transpose(bank("F", a * P, (a + 1) * P), ao[:, a * P:(a + 1) * P], ident)
                    give("F", "act", ins)

            def ffn():
                eng.wait_ge(sems["h_ready"], st.seen("h_ready", KT))
                for n in FF_CHUNKS:
                    units(n)
                    take(*GROUPS)
                    eng.wait_ge(sems["a_ready"], st.seen("a_ready", n))

                    def down(f, first, last):
                        slot = st.count["weights_ready"] % 2
                        eng.wait_ge(sems["weights_ready"], st.seen("weights_ready"))
                        for m in range(KT):
                            for j, (w, part) in enumerate(PARTS):
                                src = (a_hi, a_lo)[part]
                                rhs = src[:, f, :] if isinstance(f, int) else src[:, ds(f, 1), :].rearrange(
                                    "p o c -> p (o c)")
                                ins = mm(psum[:, m * 512:(m + 1) * 512], w[:, slot, m * P:(m + 1) * P], rhs,
                                         first and j == 0, last and j == 2)
                        ins.then_inc(sems["unit_done"], st.made("unit_done"))

                    down(0, True, False)
                    down(1, False, False)
                    with st.loop(n // 2 - 2, weights_ready=2, unit_done=2) as i:
                        down(i * 2 + 2, False, False)
                        down(i * 2 + 3, False, False)
                    down(n - 2, False, False)
                    down(n - 1, False, True)

            eng.wait_ge(sems["const_loaded"], 48)
            for name, n in CREDIT.items():
                eng.sem_inc(sems[name], n)
            take("E")
            give("E", "act", mm(bank("E", 0, 384)[0:HEADS, :], rel_b[:, :],
                                table("buckets")[0:BUCKETS, :], True, True))
            for t in range(NB):
                g = "CD"[t % 2]
                eng.wait_ge(sems[f"xtok_loaded{t % 2}"], st.seen(f"xtok_loaded{t % 2}", 16))
                take(g)
                for k in range(KT):
                    ins = eng.transpose(bank(g, k * P, (k + 1) * P), xtok[:, t % 2, k * P:(k + 1) * P], ident)
                give(g, "dve", ins)
            eng.wait_ge(sems["ident_ready"], st.seen("ident_ready", 2))
            with st.layers():
                norm()
                proj()
                retention(0)
                scores(0)
                norm()
                proj()
                retention(1)
                s5()
                scores(1)
                for h in range(2):
                    attend(h)
                    eng.wait_ge(sems["mix_ready"], st.seen("mix_ready", TT + 1))
                    units(4)
                    norm()
                    ffn()
            for h in range(2):
                norm()
                eng.wait_ge(sems["fin_ready"], st.seen("fin_ready"))
                for t in range(TT):
                    g = "CD"[t % 2]
                    take(g)
                    for k in range(KT):
                        ins = eng.transpose(bank(g, k * P, (k + 1) * P), x_T[:, k, t * P:(t + 1) * P], ident)
                    give(g, "dve", ins)


_INS = ['x', 'w_in', 'w_out', 'norm_mix', 'ssm_a_re', 'ssm_a_im', 'ssm_log_dt', 'ssm_b_re', 'ssm_b_im',
        'ssm_c_re', 'ssm_c_im', 'ssm_d', 'ssm_glu_w', 'ssm_glu_b', 'rel_bias', 'ret_gn', 'norm_ffn',
        'w_ffn_in', 'w_ffn_out', 'norm_final']


def kernel(**inputs):
    import numpy as _np
    import concourse.bacc as _bacc
    from concourse import mybir as _mybir
    from concourse.bass_utils import run_bass_kernel_spmd as _run

    nc = _bacc.Bacc("TRN2", target_bir_lowering=False, num_devices=1)
    arrays, args = {}, []
    for name in _INS:
        a = _np.ascontiguousarray(inputs[name])
        arrays[f"in_{name}_dram"] = a
        args.append(nc.dram_tensor(f"in_{name}_dram", a.shape, _mybir.dt.from_np(a.dtype), kind="ExternalInput").ap())
    tables, at = constants()
    arrays["tables_dram"] = tables
    args.append(nc.dram_tensor("tables_dram", tables.shape, _mybir.dt.float32, kind="ExternalInput").ap())
    args.append(nc.dram_tensor("out_0_dram", (1, T, D), _mybir.dt.float32, kind="ExternalOutput").ap())
    build_trunk(nc, *args, at)
    r = _run(nc, [arrays], core_ids=[0])
    return r.results[0]["out_0_dram"]
```

```python
from contextlib import ExitStack, contextmanager

import numpy as np

import concourse.bass as bass
from concourse import mybir

ALU = mybir.AluOpType
ACTF = mybir.ActivationFunctionType
F32 = mybir.dt.float32
F32R = mybir.dt.float32r
BF16 = mybir.dt.bfloat16
AX_X = mybir.AxisListType.X
ds = bass.ds

P = 128
T, D, DEPTH = 1024, 1024, 2
HALF = 512
KT = D // P
TT = HALF // P
NB = T // P
D_FF = 2816
FT = D_FF // P
FF_CHUNKS = (8, 8, 6)
TOPK = 256
HEADS, DH = 8, 64
IDX_HEADS = 4
RH = 4
BUCKETS = 32
EPS = 1e-6
NONCAUSAL = -1e38
TAKEN = -3e38
MASKED = -1e31
S5_STEPS = 8
S5_CHUNKS = T // S5_STEPS

C_U, C_Q, C_K, C_V, C_IQ, C_IK, C_IW, C_RET = 0, 256, 768, 832, 896, 1152, 1216, 1220
CM_U, CM_Q, CM_IQ, CM_K, CM_IK, CM = 0, 2, 6, 8, 9, 10

UNITS_PROJ = CM + 1 + 8
UNITS_OUT = 8
UNITS_FFN = 3 * FT
UNITS = 2 * (UNITS_PROJ + UNITS_OUT + UNITS_FFN)

GROUPS = {"A": (0, 1), "B": (1, 1), "C": (2, 2), "D": (4, 2), "E": (6, 1), "F": (7, 1)}

EARLY = ((((5, 3),), ((6, 12),)), (((6, 2), (7, 1)), ((6, 4), (7, 8))), (((7, 2),), ((7, 4),)))

NORM_STEPS = ((2, 4), (4, 6), (6, 7), (7, 8))

CREDIT = {"unit_done": 2, "weights_ready": 2, "relu_used": 2, "gate_used": 1, "square_used": 1}
CREDIT.update({f"{g}_free": 1 for g in GROUPS})


class Counts:

    def __init__(self, eng, name, held=None):
        self.eng, self.name, self.held = eng, name, held
        self.count = {}
        self.loops = []

    def value(self, sem, n):
        v = n + CREDIT.get(sem, 0)
        for reg, per in self.loops:
            if per.get(sem, 0):
                v = reg * per[sem] + v
        return v

    def add(self, sem, n=1):
        self.count[sem] = self.count.get(sem, 0) + n
        return self.count[sem]

    def seen(self, sem, n=1):
        return self.value(sem, self.add(sem, n))

    def taken(self, sem):
        return self.value(sem, self.add(sem)) - CREDIT[sem]

    def made(self, sem, n=1):
        self.add(sem, n)
        return n

    def now(self, sem):
        return self.value(sem, self.count[sem])

    @contextmanager
    def loop(self, times, **per):
        before = dict(self.count)
        if self.held is not None:
            self.eng.sem_inc(self.held, 1)
        with self.eng.Fori(0, times) as i:
            self.loops.append((i, per))
            yield i
            self.loops.pop()
        did = {s: n - before.get(s, 0) for s, n in self.count.items() if n != before.get(s, 0)}
        assert did == {s: n for s, n in per.items() if n}, (self.name, did, per)
        for s, n in per.items():
            self.count[s] += n * (times - 1)


def constants():
    f = np.float32
    parts = {}
    parts["ident"] = np.eye(P, dtype=f)
    parts["ones"] = np.ones((P, P), f)
    parts["noncausal"] = np.triu(np.full((P, P), NONCAUSAL, f), 1)
    parts["quads"] = np.kron(np.eye(4, dtype=f), np.ones((32, 32), f))
    inv = (f(10000.0) ** (-np.arange(32, dtype=f) / f(32))).astype(f)
    ang = (np.arange(T, dtype=f)[:, None] * inv[None, :]).astype(f).astype(np.float64)
    for n, fn in (("cos", np.cos), ("sin", np.sin)):
        parts[n] = fn(ang).astype(f).reshape(NB, P, 32).transpose(1, 0, 2).reshape(P, NB * 32)
    gamma = 1.0 - 2.0 ** (-5.0 - np.arange(RH, dtype=np.float64))
    lg = np.log(gamma)
    i = np.arange(P, dtype=np.float64)
    diff = i[None, :] - i[:, None]
    dec = np.where(diff[None] >= 0, np.exp(lg[:, None, None] * np.maximum(diff, 0.0)[None]), 0.0)
    parts["decay"] = (dec * 0.125).astype(f).transpose(1, 0, 2).reshape(P, RH * P)
    parts["wk"] = (np.exp(lg[None, :] * (P - 1.0 - i)[:, None]) * 0.125).astype(f)
    wq = np.exp(lg[:, None] * (i + 1.0)[None, :])
    parts["wq"] = np.stack([np.repeat(wq[2 * t:2 * t + 2], 64, axis=0) for t in range(2)], 1).astype(f).reshape(P, 2 * P)
    gc = np.exp(lg * P)
    parts["gchunk"] = np.stack([np.repeat(gc[2 * t:2 * t + 2], 64) for t in range(2)], 1).astype(f)
    dist = np.maximum(255 - np.arange(384), 0)
    nf = np.maximum(dist, 1).astype(f)
    large = 16 + (np.log(nf / f(16)).astype(f) / f(np.log(8.0)) * f(16)).astype(np.int32)
    bucket = np.where(dist < 16, dist, np.minimum(large, BUCKETS - 1))
    hot = np.zeros((P, 384), f)
    hot[bucket, np.arange(384)] += 1.0
    hot[BUCKETS - 1, :] -= 1.0
    parts["buckets"] = hot
    at, n = {}, 0
    for k, a in parts.items():
        at[k] = (n, a.shape[1])
        n += a.shape[1]
    return np.ascontiguousarray(np.concatenate(list(parts.values()), 1)), at


def build_trunk(nc, x, w_in, w_out, norm_mix, a_re, a_im, log_dt, b_re, b_im, c_re, c_im, ssm_d, glu_w,
                glu_b, rel_bias, ret_gn, norm_ffn, w_ffn_in, w_ffn_out, norm_final, const, out, at):
    ctx = ExitStack()
    with ctx:
        def sb(name, shape, dt=F32, where=None):
            return (where or ctx).enter_context(nc.sbuf_tensor(name, shape, dt))

        cst = sb("cst", [P, const.shape[1]])

        def table(name):
            o, n = at[name]
            return cst[:, o:o + n]

        ident = table("ident")
        h_hi = sb("h_hi", [P, KT, HALF], F32R)
        h_lo = sb("h_lo", [P, KT, HALF], F32R)
        w_raw = sb("w_raw", [P, 2, 1024])
        w_hi = sb("w_hi", [P, 2, 1024], F32R)
        w_lo = sb("w_lo", [P, 2, 1024], F32R)
        cm = sb("cm", [P, CM - 2, T])
        iq = sb("iq", [P, 2, HALF])
        vw = sb("vw", [P, NB, P])
        ret_T = sb("ret_T", [P, 2, T])
        x_T = sb("x_T", [P, KT, HALF])
        bias_win = sb("bias_win", [P, HEADS, 256])
        NK = [P * (b + 1) for b in range(NB)]
        score = {b: sb(f"score{b}", [P, NK[b]]) for b in (2, 3)}
        ident_b = sb("ident_b", [P, P], BF16)
        causal_b = sb("causal_b", [P, P], BF16)
        gains = sb("gains", [P, 2 * DEPTH + 1, KT])
        gn_row = sb("gn_row", [P, 256])
        s5p = sb("s5p", [P, 64, 8])
        s5_glu = sb("s5_glu", [P, 2, 256])
        s5_col = sb("s5_col", [P, 2, 2])
        rel_b = sb("rel_b", [BUCKETS, HEADS])
        top8 = sb("top8", [P, 8])
        act_one = sb("act_one", [P, 1])
        s5_ct = sb("s5_ct", [P, 2, 8, 32])
        s5_bb = sb("s5_bb", [P, 2, 8, 16])
        tok4 = sb("tok4", [P, TT])
        nmax = sb("nmax", [P, HEADS])
        rsum = sb("rsum", [P, HEADS])
        rinv = sb("rinv", [P, HEADS])
        gsum = sb("gsum", [P, 4, TT * RH])
        state = sb("state", [P, 2, 2, 64])

        def shared(size, *stages):
            got = {}
            for tensors in stages:
                with ExitStack() as stage:
                    for name, shape, dt in tensors:
                        got[name] = sb(name, shape, dt, stage)
            sb(f"shared{size}", [P, size])
            return got

        big = shared(
            11776,
            [("a_hi", [P, 8, HALF], F32R), ("a_lo", [P, 8, HALF], F32R)]
            + [(f"score{b}", [P, NK[b]], F32) for b in range(4, NB)],
            [("r_in", [P, TT, 4, 256], F32), ("rot", [P, TT, 2, 256], F32), ("rtmp", [P, 2, 1024], F32),
             ("rqT", [P, 2, HALF], F32), ("rkT", [P, 2, HALF], F32)],
            [("Vt", [P, 8, 2, P], F32), ("Yt", [P, 2, 8, 4, 32], F32),
             ("Kt", [P, 8, P], F32), ("Et", [P, 2, 4, P], F32), ("Gt", [P, 2, 4, P], F32),
             ("Ht", [P, 2, 4, P], F32), ("Z", [P, 2, 8, 4, 32], F32), ("Xt", [P, 2, 512], F32)],
            [("prob", [P, 2, 1024], F32), ("probT", [P, 2, 1024], F32), ("ao", [P, 512], F32)],
            [("xtok", [P, 2, D], F32), ("brow", [HEADS, 384], F32)],
        )
        small = shared(
            2560,
            [("rstd", [P, HALF], F32), ("ntmp", [P, 4, HALF], F32)],
            [("rstd_", [P, HALF], F32), ("ntmp_", [P, 2, HALF], F32), ("gate", [P, HALF], F32),
             ("atmp", [P, HALF], F32)],
            [("relu", [P, 2, 1024], F32)],
            [("norm_part", [P, 3 * HALF], F32), ("relu_short", [P, 2, HALF], F32)],
            [("sums_part", [P, 2 * HALF], F32), ("s5_b", [P, 2, 8, 16], F32), ("s5_c", [P, 2, 2, P], F32),
             ("s5_t", [P, 2, 8, 16], F32)],
        )
        a_hi, a_lo = big["a_hi"], big["a_lo"]
        score.update({b: big[f"score{b}"] for b in range(4, NB)})
        r_in, rot, rtmp, rqT, rkT = (big[n] for n in ("r_in", "rot", "rtmp", "rqT", "rkT"))
        Z, Vt, Yt, Kt, Et, Gt, Ht, Xt = (big[n] for n in ("Z", "Vt", "Yt", "Kt", "Et", "Gt", "Ht", "Xt"))
        prob, probT, ao, xtok, brow = (big[n] for n in ("prob", "probT", "ao", "xtok", "brow"))
        ntmp, rstd, relu, relu_short = (small[n] for n in ("ntmp", "rstd", "relu", "relu_short"))
        square = ntmp[:, 0, :]
        x_next = cm[:, 0:4, :].rearrange("p a (b c) -> p (a b) c", b=2)
        s5_b, s5_c, s5_t = (small[n] for n in ("s5_b", "s5_c", "s5_t"))
        gate, atmp = small["gate"], small["atmp"]

        psum = ctx.enter_context(nc.psum_tensor("psum", [P, 4096], F32))
        x_dram = nc.dram_tensor("x_half", [2, P, KT * HALF], F32).ap()
        bias_dram = nc.dram_tensor("bias_rows", [HEADS, P, 384], F32).ap()

        def bank(group, a=0, b=None):
            first, n = GROUPS[group]
            return psum[:, first * 512 + a:first * 512 + (n * 512 if b is None else b)]

        names = ["raw_loaded0", "raw_loaded1", "hi_ready", "weights_ready", "unit_done", "square_ready",
                 "square_used", "sum_ready", "diag_ready", "mean_ready", "rstd_ready", "norm_tmp",
                 "h_hi_ready", "h_ready", "x_loaded", "x_stored", "x_updated", "params_loaded", "s5_loaded",
                 "params_used", "next_loaded", "const_loaded", "xtok_loaded0", "xtok_loaded1",
                 "bias_stored", "bias_loaded", "ident_ready", "cm_ready", "qk_in", "ret_in", "relu_ready",
                 "relu_used", "mask_ready", "nmax_ready", "p_ready", "ptA_ready", "ptB_ready", "ao_ready",
                 "mix_hi_ready", "mix_ready", "gate_ready", "gate_used", "a_ready", "out_stored0",
                 "out_stored1", "rot_ready", "rT_ready", "qs_ready", "st_ready", "o_ready", "state_ready",
                 "gvar_ready", "gstd_ready", "ret_out", "retT_ready", "silu_ready", "dt_ready",
                 "angle_ready", "trig_ready", "z_ready", "vt_ready", "v_ready", "hprev_ready", "kt_ready",
                 "y_ready", "sig_ready", "y_gated", "xtok_used", "fin_ready", "fin_out", "act_chain",
                 "dve_chain", "dve_held", "pe_held", "round_step"]
        for g in GROUPS:
            names += [f"{g}_free", f"{g}_to_act", f"{g}_to_dve"]
        sems = {n: ctx.enter_context(nc.semaphore(n)) for n in names}
        block = ctx.enter_context(nc.Block())

        rows = w_in.rearrange("l (k p) c -> p l k c", p=P)
        rows_out = w_out.rearrange("l (k p) c -> p l k c", p=P)
        rows_gu = w_ffn_in.rearrange("l (k p) c -> p l k c", p=P)
        rows_down = w_ffn_out.rearrange("l (k p) c -> p l k c", p=P)

        @block.sync
        def _(eng):
            st = Counts(eng, "sp")
            eng.dma_start(cst[:, :], const).then_inc(sems["const_loaded"], 16)
            for dst, src in ((gains[:, 0:DEPTH, :], norm_mix.rearrange("l (k p) -> p l k", p=P)),
                             (gains[:, DEPTH:2 * DEPTH, :], norm_ffn.rearrange("l (k p) -> p l k", p=P)),
                             (gains[:, 2 * DEPTH, :], norm_final.rearrange("(k p) -> p k", p=P))):
                eng.dma_start(dst, src, allow_slow_non_contiguous=True).then_inc(sems["const_loaded"], 16)
            eng.dma_start(rel_b[:, :], rel_bias).then_inc(sems["const_loaded"], 16)

            def load_unit(width, *sources):
                u = st.add("weights_ready") - 1
                eng.wait_ge(sems["weights_ready"], st.value("weights_ready", u + 1) - 2)
                dst = w_raw[:, u % 2, :].rearrange("p (k c) -> p k c", c=width)
                a = 0
                for src in sources:
                    w = src.shape[-1]
                    ins = eng.dma_start(dst[:, :, a:a + w], src.rearrange("p l k c -> p (l k) c"))
                    ins.then_inc(sems[f"raw_loaded{u % 2}"], st.made(f"raw_loaded{u % 2}", 16))
                    a += w

            def proj(l):
                with st.loop(3, weights_ready=2, raw_loaded0=16, raw_loaded1=16) as i:
                    for e in range(2):
                        load_unit(P, rows[:, ds(l, 1), :, ds(i * 256 + e * P, P)])
                for e in range(2):
                    load_unit(P, rows[:, ds(l, 1), :, C_IQ + e * P:C_IQ + (e + 1) * P])
                for c in (C_K, C_IK):
                    one = rows[:, ds(l, 1), :, c:c + 64]
                    load_unit(P, one, one)
                load_unit(P, rows[:, ds(l, 1), :, C_V:C_V + 64], rows[:, ds(l, 1), :, C_IW:C_IW + 64])
                for n in range(2):
                    for j in range(4):
                        c = C_RET + n * 512
                        load_unit(512, rows[:, ds(l, 1), 2 * j:2 * j + 2, c:c + 512])

            def mix_out(l):
                with st.loop(4, weights_ready=2, raw_loaded0=16, raw_loaded1=16) as i:
                    for e in range(2):
                        load_unit(P, rows_out[:, ds(l, 1), :, ds(i * 256 + e * P, P)])

            def ffn(l):
                f0 = 0
                for n in FF_CHUNKS:
                    with st.loop(n, weights_ready=2, raw_loaded0=16, raw_loaded1=16) as i:
                        load_unit(P, rows_gu[:, ds(l, 1), :, ds(i * P + f0 * P, P)])
                        load_unit(P, rows_gu[:, ds(l, 1), :, ds(i * P + (D_FF + f0 * P), P)])
                    with st.loop(n // 2, weights_ready=2, raw_loaded0=16, raw_loaded1=16) as i:
                        for e in range(2):
                            load_unit(D, rows_down[:, ds(l, 1), ds(i * 2 + (f0 + e), 1), :])
                    f0 += n

            def params(l):
                def par(dst, src):
                    eng.dma_start(dst, src, allow_slow_non_contiguous=True).then_inc(sems["params_loaded"], st.made("params_loaded", 16))

                lay = ds(l, 1)
                par(gn_row[:, :], ret_gn[lay, :].to_broadcast([P, 256]))
                par(s5_glu[:, :, :], glu_w[lay, :, :].rearrange("l (k p) c -> p (l k) c", p=P))
                par(s5_col[:, 0, :], ssm_d[lay, :, :].rearrange("l (h g) p -> (l g p) h", h=2))
                par(s5_col[:, 1, :], glu_b[lay, :].rearrange("l (h p) -> p (l h)", h=2))
                for r in range(2):
                    half = slice(64 * r, 64 * r + 64)
                    par(s5p[half, 0, :], a_re[lay, r::2, :].rearrange("l q n -> n (l q)"))
                    par(s5p[half, 1, :], a_im[lay, r::2, :].rearrange("l q n -> n (l q)"))
                    par(s5p[half, 2, :], log_dt[lay, r::2].to_broadcast([64, 8]))
            for l in range(DEPTH):
                if l == 0:
                    params(0)
                for h in range(2):
                    proj(l)
                for h in range(2):
                    mix_out(l)
                    if h == 0 and l + 1 < DEPTH:
                        eng.wait_ge(sems["params_used"], l + 1)
                        params(l + 1)
                    ffn(l)

        @block.gpsimd
        def _(eng):
            st = Counts(eng, "pool")
            eng.wait_ge(sems["const_loaded"], 80)

            def weight_lo():
                u = st.count.get("weights_ready", 0) % 2
                eng.wait_ge(sems["hi_ready"], st.seen("hi_ready"))
                eng.tensor_tensor(w_lo[:, u, :], w_raw[:, u, :], w_hi[:, u, :].bitcast(F32), ALU.subtract).then_inc(
                    sems["weights_ready"], st.made("weights_ready"))

            def weights(n):
                with st.loop(n // 2, hi_ready=2, weights_ready=2):
                    for _ in range(2):
                        weight_lo()
                if n % 2:
                    weight_lo()

            def h_lows(first=0, last=KT):
                for k in range(first, last):
                    eng.wait_ge(sems["h_hi_ready"], st.seen("h_hi_ready"))
                    eng.tensor_tensor(h_lo[:, k, :], ntmp[:, k % 4, :], h_hi[:, k, :].bitcast(F32),
                                      ALU.subtract).then_inc(sems["h_ready"], st.made("h_ready"))

            weights(2)
            h_lows()
            for l in range(DEPTH):
                weights(UNITS_PROJ)
                h_lows()
                weights(UNITS_PROJ + UNITS_OUT)
                h_lows()
                weights(UNITS_FFN + UNITS_OUT)
                h_lows()
                weights(UNITS_FFN - 6)
                if l + 1 < DEPTH:
                    for k in range(0, KT, 2):
                        h_lows(k, k + 2)
                        weight_lo()
                    weights(2)
                else:
                    weights(4)

        @block.scalar
        def _(eng):
            st = Counts(eng, "act")

            def link(ins):
                ins.then_inc(sems["act_chain"], st.made("act_chain"))
                eng.wait_ge(sems["act_chain"], st.now("act_chain"))

            act = eng.activation

            def prep(pieces=1):
                u = st.add("hi_ready") - 1
                eng.wait_ge(sems["unit_done"], st.value("unit_done", u + 1) - 2)
                eng.wait_ge(sems[f"raw_loaded{u % 2}"], st.seen(f"raw_loaded{u % 2}", 16 * pieces))
                ins = act(w_hi[:, u % 2, :], w_raw[:, u % 2, :], ACTF.Copy)
                ins.then_inc(sems["hi_ready"], 1)

            def load_x(h):
                eng.dma_start(x_T[:, :, :], x_dram[h].rearrange("p (k c) -> p k c", k=KT)).then_inc(
                    sems["x_loaded"], st.made("x_loaded", 16))

            def store_x(h, src):
                eng.dma_start(x_dram[h].rearrange("p (k c) -> p k c", k=KT), src).then_inc(
                    sems["x_stored"], st.made("x_stored", 16))

            def squares(x_tile):
                eng.wait_ge(sems["square_used"], st.taken("square_used"))
                act(square, x_tile, ACTF.Square).then_inc(sems["square_ready"], st.made("square_ready"))

            def root():
                act(act_one[:, :], table("ones")[:, 0:1], ACTF.Sqrt)
                eng.wait_ge(sems["mean_ready"], st.seen("mean_ready"))
                act(tok4[:, :], tok4[:, :], ACTF.Sqrt).then_inc(sems["rstd_ready"], st.made("rstd_ready"))

            def h_highs(first=0, last=KT):
                for k in range(first, last):
                    eng.wait_ge(sems["norm_tmp"], st.seen("norm_tmp"))
                    act(h_hi[:, k, :], ntmp[:, k % 4, :], ACTF.Copy).then_inc(
                        sems["h_hi_ready"], st.made("h_hi_ready"))
                    st.add("h_ready")

            def channel_unit(h, i):
                cols = slice(h * HALF, (h + 1) * HALF)
                dst = iq[:, i - 6, :] if i in (6, 7) else cm[:, i if i < 6 else i - 2, cols]
                g = "AB"[i % 2]
                eng.wait_ge(sems["unit_done"], st.seen("unit_done"))
                act(dst, bank(g), ACTF.Copy, scale=DH ** -0.5 if i == CM_K else 1.0).then_inc(
                    sems[f"{g}_free"], st.made(f"{g}_free"))
                prep(2 if i in (6, 7, 8) else 1)

            def s5_angles():
                mag, mag8, sin1, cos1 = (s5p[:, i, :] for i in (7, 8, 9, 10))
                adt, ang, cosarg = (s5p[:, i, :] for i in (4, 5, 6))
                eng.wait_ge(sems["angle_ready"], st.seen("angle_ready"))
                act(mag, adt, ACTF.Exp)
                act(mag8, adt, ACTF.Exp, scale=float(S5_STEPS))
                act(sin1, ang, ACTF.Sin)
                act(cos1, cosarg, ACTF.Sin).then_inc(sems["trig_ready"], st.made("trig_ready"))

            def proj(h, l):
                if h == 0:
                    eng.wait_ge(sems["h_ready"], st.now("h_ready"))
                    load_s5(l)
                    act(s5p[:, 3, :], s5p[:, 2, :], ACTF.Exp).then_inc(sems["dt_ready"], st.made("dt_ready"))
                for i in range(0 if h == 0 else 2, CM):
                    channel_unit(h, i)
                    if h == 0 and i < KT:
                        squares(x_T[:, i, :])
                    if h == 0 and i == 1:
                        s5_angles()
                if h == 0:
                    root()
                eng.wait_ge(sems["unit_done"], st.seen("unit_done"))
                link(act(vw[:, TT * h:TT * (h + 1), :], bank("E").rearrange("p (t c) -> p t c", t=TT),
                            ACTF.Copy))
                eng.sem_inc(sems["E_free"], 1)
                eng.sem_inc(sems["cm_ready"], 1)
                prep()
                for n in range(2):
                    for j in range(4):
                        eng.wait_ge(sems["unit_done"], st.seen("unit_done"))
                        prep()
                    if n == 0:
                        for t, g in enumerate("CD"):
                            link(act(r_in[:, 2 * t:2 * t + 2, 0:2, :].rearrange("p t a c -> p t (a c)"),
                                     bank(g).rearrange("p (t c) -> p t c", t=2), ACTF.Copy))
                            eng.sem_inc(sems[f"{g}_free"], 1)
                        eng.sem_inc(sems["qk_in"], 1)
                    else:
                        for t, g in ((2, "A"), (3, "B"), (0, "E"), (1, "F")):
                            link(act(r_in[:, t, 2:4, :].rearrange("p a c -> p (a c)"), bank(g), ACTF.Copy))
                            eng.sem_inc(sems[f"{g}_free"], 1)
                eng.sem_inc(sems["ret_in"], 1)

            def scores(h):
                if h == 0:
                    eng.wait_ge(sems["h_ready"], st.now("h_ready"))
                for b in range(max(2, TT * h), TT * (h + 1)):
                    for i in range(IDX_HEADS):
                        g = "CD"[i % 2]
                        eng.wait_ge(sems[f"{g}_to_act"], st.seen(f"{g}_to_act"))
                        eng.wait_ge(sems["relu_used"], st.taken("relu_used"))
                        act((relu_short, relu)[h][:, i % 2, 0:NK[b]], bank(g, 0, NK[b]), ACTF.Relu).then_inc(sems["relu_ready"], st.made("relu_ready"))
                eng.wait_ge(sems["relu_used"], st.now("relu_used"))

            def retention(h):
                eng.wait_ge(sems["A_to_act"], st.seen("A_to_act"))
                act(rqT[:, 0, :], bank("A"), ACTF.Copy).then_inc(sems["A_free"], st.made("A_free"))
                eng.wait_ge(sems["B_to_act"], st.seen("B_to_act"))
                act(rqT[:, 1, :], bank("B"), ACTF.Copy).then_inc(sems["B_free"], st.made("B_free"))
                eng.wait_ge(sems["C_to_act"], st.seen("C_to_act"))
                link(act(rkT[:, :, :], bank("C").rearrange("p (a c) -> p a c", a=2), ACTF.Copy))
                eng.sem_inc(sems["C_free"], 1)
                eng.sem_inc(sems["rT_ready"], 1)
                if h == 0:
                    h_highs(0, 2)
                for c in range(TT):
                    eng.wait_ge(sems["D_to_act"], st.seen("D_to_act"))
                    out4 = r_in[:, c, 0, :].rearrange("p (a r e) -> p a r e", a=2, r=2)
                    for r in range(2):
                        ins = act(out4[:, :, r, :],
                                  bank("D", 512 * r, 512 * r + 128).rearrange("p (a e) -> p a e", a=2),
                                  ACTF.Copy)
                    link(ins)
                    eng.sem_inc(sems["D_free"], 1)
                    if h == 0:
                        h_highs(*NORM_STEPS[c])
                eng.sem_inc(sems["o_ready"], 1)
                link(act(r_in[:, :, 3, :], r_in[:, :, 3, :], ACTF.Silu))
                eng.sem_inc(sems["silu_ready"], 1)
                eng.wait_ge(sems["gvar_ready"], st.seen("gvar_ready"))
                act(gsum[:, 2, :], gsum[:, 2, :], ACTF.Sqrt).then_inc(sems["gstd_ready"], st.made("gstd_ready"))
                if h == 0:
                    for i in range(2):
                        channel_unit(1, i)
                eng.wait_ge(sems["C_to_act"], st.seen("C_to_act"))
                link(act(ret_T[:, :, h * HALF:(h + 1) * HALF],
                            bank("C").rearrange("p (a c) -> p a c", a=2), ACTF.Copy))
                eng.sem_inc(sems["retT_ready"], 1)
                eng.sem_inc(sems["C_free"], 1)

            def load_s5(l):
                lay = ds(l, 1)

                def par(dst, src):
                    eng.dma_start(dst, src).then_inc(sems["s5_loaded"], st.made("s5_loaded", 16))

                for r in range(2):
                    half = slice(64 * r, 64 * r + 64)
                    par(s5_b[half, 0, :, :], b_re[lay, r::2, :, :].rearrange("l q n p -> n (l q) p"))
                    par(s5_b[half, 1, :, :], b_im[lay, r::2, :, :].rearrange("l q n p -> n (l q) p"))
                    par(s5_c[:, 0, :, 64 * r:64 * r + 64],
                        c_re[lay, :, :, :].rearrange("l (h g) p n -> (l g p) h n", h=2))
                    par(s5_c[:, 1, :, 64 * r:64 * r + 64],
                        c_im[lay, :, :, :].rearrange("l (h g) p n -> (l g p) h n", h=2))

            def s5():
                for hh in range(2):
                    for c, g in enumerate("CD"):
                        eng.wait_ge(sems[f"{g}_to_act"], st.seen(f"{g}_to_act"))
                        link(act(Vt[:, :, c, :], bank(g).rearrange("p (m s) -> p m s", m=8), ACTF.Copy))
                        eng.sem_inc(sems[f"{g}_free"], 1)
                    eng.sem_inc(sems["vt_ready"], 1)
                    for q, g in enumerate("ABCD"):
                        eng.wait_ge(sems[f"{g}_to_act"], st.seen(f"{g}_to_act"))
                        ins = act(Ht[:, :, q, :], bank(g, 0, 256).rearrange("p (c s) -> p c s", c=2),
                                  ACTF.Copy)
                        if q < 3:
                            ins.then_inc(sems[f"{g}_free"], st.made(f"{g}_free"))
                    link(ins)
                    eng.sem_inc(sems["D_free"], 1)
                    eng.sem_inc(sems["v_ready"], 1)
                    eng.wait_ge(sems["C_to_act"], st.seen("C_to_act"))
                    link(act(cm[:, hh, :].rearrange("p (c j) -> p j c", j=8),
                                bank("C").rearrange("p (j c) -> p j c", j=8), ACTF.Gelu_apprx_tanh))
                    eng.sem_inc(sems["C_free"], 1)
                    eng.sem_inc(sems["y_ready"], 1)
                for n in range(2):
                    for m in range(2):
                        g = "EFAB"[2 * n + m]
                        eng.wait_ge(sems[f"{g}_to_act"], st.seen(f"{g}_to_act"))
                        ins = act(Z2[:, m, n * HALF:(n + 1) * HALF], bank(g), ACTF.Sigmoid,
                                  bias=s5_col[:, 1, m:m + 1])
                        if 2 * n + m < 3:
                            ins.then_inc(sems[f"{g}_free"], st.made(f"{g}_free"))
                link(ins)
                eng.sem_inc(sems["B_free"], 1)
                eng.sem_inc(sems["sig_ready"], 1)

            Z2 = Z[:, :, :, :, :].rearrange("p a m q r -> p (a m q r)").rearrange("p (m t) -> p m t", m=2)

            def attend(h):
                for b in range(TT * h, TT * (h + 1)):
                    nk = NK[b]

                    def copies(i):
                        if b >= 4 or i % 2 == 0:
                            eng.wait_ge(sems["A_to_act"], st.seen("A_to_act"))
                            n = min(b + 1, 4) * P
                            act(probT[:, i % 2, 0:n], bank("A", 0, n), ACTF.Copy).then_inc(sems["ptA_ready"], st.made("ptA_ready"))

                    for i in range(HEADS):
                        g = "CD"[i % 2]
                        eng.wait_ge(sems["nmax_ready"], st.seen("nmax_ready"))
                        act(prob[:, i % 2, 0:nk], bank(g, 0, nk), ACTF.Exp,
                                                 bias=nmax[:, i:i + 1], accum_out=rsum[:, i:i + 1]).then_inc(sems["p_ready"], st.made("p_ready"))
                        if i >= 1:
                            copies(i - 1)
                    copies(HEADS - 1)
                    eng.wait_ge(sems["F_to_act"], st.seen("F_to_act"))
                    o = (b % TT) * P
                    act(h_hi[:, 2:6, o:o + P],
                                                  bank("F").rearrange("p (a c) -> p a c", a=4), ACTF.Copy).then_inc(sems["mix_hi_ready"], st.made("mix_hi_ready"))
                    if b % TT == 0:
                        cols = slice(h * HALF, (h + 1) * HALF)
                        if h == 0:
                            eng.wait_ge(sems["y_gated"], st.seen("y_gated"))
                        act(h_hi[:, 0:2, :], cm[:, 0:2, cols], ACTF.Copy)
                        act(h_hi[:, 6:8, :], ret_T[:, :, cols], ACTF.Copy).then_inc(
                            sems["mix_hi_ready"], st.made("mix_hi_ready"))
                        if h == 1:
                            eng.wait_ge(sems["x_stored"], st.now("x_stored"))
                            load_x(1)

            def mix_out():
                with st.loop(4, unit_done=2, hi_ready=2, raw_loaded0=16, raw_loaded1=16, x_updated=2,
                             square_used=2, square_ready=2) as i:
                    for e in range(2):
                        st.add("unit_done")
                        prep()
                        eng.wait_ge(sems["x_updated"], st.seen("x_updated"))
                        squares(x_T[:, ds(i * 2 + e, 1), :].rearrange("p o c -> p (o c)"))
                root()
                h_highs()

            def ffn(l, h):
                for c, n in enumerate(FF_CHUNKS):
                    last_chunk = c == len(FF_CHUNKS) - 1
                    sums = h == 1 and c == 1
                    if sums:
                        eng.wait_ge(sems["next_loaded"], st.now("next_loaded"))
                    def gates(i):
                        st.add("unit_done")
                        prep()
                        eng.wait_ge(sems["unit_done"], st.now("unit_done"))
                        eng.wait_ge(sems["gate_used"], st.taken("gate_used"))
                        ins = act(gate[:, :], bank("A"), ACTF.Silu)
                        ins.then_inc(sems["gate_ready"], st.made("gate_ready"))
                        eng.wait_ge(sems["gate_ready"], st.now("gate_ready"))
                        eng.sem_inc(sems["A_free"], 1)
                        st.add("unit_done")
                        if sums:
                            squares(x_next[:, ds(i, 1), :].rearrange("p o c -> p (o c)"))
                        prep()

                    early_mean = h == 1 and last_chunk
                    with st.loop(n - early_mean, unit_done=2, hi_ready=2, raw_loaded0=16, raw_loaded1=16,
                                 gate_used=1, gate_ready=1, square_used=int(sums), square_ready=int(sums)) as i:
                        gates(i)
                    if early_mean:
                        root()
                        gates(n - 1)
                    if h == 1 and last_chunk:
                        for j in range(n):
                            if l + 1 < DEPTH:
                                h_highs(min(2 * j, KT), min(2 * j + 2, KT))
                            st.add("unit_done")
                            if j < n - 2 or l + 1 < DEPTH:
                                prep()
                    else:
                        with st.loop(n // 2, unit_done=2, hi_ready=2, raw_loaded0=16, raw_loaded1=16):
                            for _ in range(2):
                                st.add("unit_done")
                                prep()

            eng.wait_ge(sems["const_loaded"], 80)
            act(ident_b[:, :], ident, ACTF.Copy).then_inc(sems["ident_ready"], st.made("ident_ready"))
            eng.wait_ge(sems["E_to_act"], st.seen("E_to_act"))
            link(act(brow[:, :], bank("E", 0, 384)[0:HEADS, :], ACTF.Copy))
            eng.sem_inc(sems["E_free"], 1)
            eng.dma_start(
                bias_dram, brow[:, :].unsqueeze(1).broadcast_to([HEADS, P, 384])).then_inc(sems["bias_stored"], st.made("bias_stored", 16))
            eng.wait_ge(sems["bias_stored"], 16)
            eng.dma_start(
                bias_win[:, :, :],
                bass.AP(tensor=bias_dram.tensor, offset=P - 1, ap=[[383, P], [P * 384, HEADS], [1, 256]])).then_inc(sems["bias_loaded"], st.made("bias_loaded", 16))
            for t in range(NB):
                if t >= 2:
                    eng.wait_ge(sems["xtok_used"], st.seen("xtok_used"))
                eng.dma_start(xtok[:, t % 2, :], x[0, t * P:(t + 1) * P, :]).then_inc(
                    sems[f"xtok_loaded{t % 2}"], st.made(f"xtok_loaded{t % 2}", 16))
            st.add("xtok_used", 2)
            prep()
            prep()
            eng.wait_ge(sems["x_updated"], st.seen("x_updated"))
            store_x(0, x_next)
            for k in range(KT):
                squares(x_next[:, k, :])
            root()
            h_highs()
            eng.wait_ge(sems["x_stored"], st.now("x_stored"))
            eng.wait_ge(sems["x_updated"], st.seen("x_updated"))
            for l in range(DEPTH):
                eng.wait_ge(sems["params_loaded"], st.seen("params_loaded", 16 * 10))
                store_x(1, x_T[:, :, :])
                proj(0, l)
                retention(0)
                scores(0)
                eng.wait_ge(sems["x_stored"], st.now("x_stored"))
                load_x(0)
                proj(1, l)
                retention(1)
                s5()
                scores(1)
                for h in range(2):
                    attend(h)
                    if h == 0:
                        eng.sem_inc(sems["params_used"], 1)
                    mix_out()
                    if h == 1:
                        eng.dma_start(x_next, x_dram[0].rearrange("p (k c) -> p k c", k=KT)).then_inc(
                            sems["next_loaded"], st.made("next_loaded", 16))
                    ffn(l, h)
                    eng.wait_ge(sems["x_updated"], st.seen("x_updated"))
                    if h == 0:
                        store_x(0, x_T[:, :, :])
            for k in range(KT):
                squares(x_T[:, k, :])
            for h in range(2):
                if h == 1:
                    root()
                for t in range(TT):
                    eng.wait_ge(sems["fin_out"], st.seen("fin_out"))
                    ins = eng.dma_start(out[0, (h * TT + t) * P:(h * TT + t + 1) * P, :], xtok[:, t % 2, :])
                    ins.then_inc(sems[f"out_stored{t % 2}"], st.made(f"out_stored{t % 2}", 16))
            for e in range(2):
                eng.wait_ge(sems[f"out_stored{e}"], 16 * TT)

        @block.vector
        def _(eng):
            st = Counts(eng, "dve", sems["dve_held"])

            def link(ins):
                ins.then_inc(sems["dve_chain"], st.made("dve_chain"))
                eng.wait_ge(sems["dve_chain"], st.now("dve_chain"))

            def hold():
                eng.sem_inc(sems["dve_held"], 1)

            tt, ts, stt = eng.tensor_tensor, eng.tensor_scalar, eng.scalar_tensor_tensor
            MUL, ADD, SUB, MAX = ALU.mult, ALU.add, ALU.subtract, ALU.max

            def add_squares():
                eng.wait_ge(sems["square_ready"], st.seen("square_ready"))
                link(tt(rstd[:, :], rstd[:, :], square, ADD))
                eng.sem_inc(sems["square_used"], 1)

            def clear_sum():
                if "norm_tmp" in st.count:
                    eng.wait_ge(sems["norm_tmp"], st.now("norm_tmp"))
                link(eng.memset(rstd[:, :], 0.0))

            def rsqrt():
                eng.sem_inc(sems["sum_ready"], 1)
                eng.wait_ge(sems["F_to_dve"], st.seen("F_to_dve"))
                link(ts(tok4[:, :], bank("F", 0, TT), 1.0 / D, EPS, MUL, ADD))
                link(eng.reciprocal(tok4[:, :], tok4[:, :]))
                eng.sem_inc(sems["mean_ready"], 1)
                eng.wait_ge(sems["rstd_ready"], st.seen("rstd_ready"))
                link(tt(rstd[:, :].rearrange("p (t c) -> p t c", t=TT),
                        ident.unsqueeze(1).broadcast_to([P, TT, P]),
                        tok4[:, :].unsqueeze(2).broadcast_to([P, TT, P]), MUL))
                eng.sem_inc(sems["diag_ready"], 1)

            def factors(keep=True):
                eng.wait_ge(sems["F_to_dve"], st.seen("F_to_dve"))
                if keep:
                    link(eng.tensor_copy(rstd[:, :], bank("F")))
                    eng.sem_inc(sems["F_free"], 1)

            def normalise(src, gain, by, first=0, last=KT):
                for k in range(first, last):
                    if k >= 4:
                        eng.wait_ge(sems["h_ready"], st.seen("h_ready"))
                    stt(ntmp[:, k % 4, :], src[:, k, :], gains[:, gain, k:k + 1], by, MUL, MUL).then_inc(
                        sems["norm_tmp"], st.made("norm_tmp"))
                if last == KT:
                    st.add("h_ready", 4)

            def scale_last(src):
                for k in range(KT):
                    ins = stt(src[:, k, :], src[:, k, :], gains[:, 2 * DEPTH, k:k + 1], rstd[:, :], MUL, MUL)
                link(ins)
                eng.sem_inc(sems["fin_ready"], 1)

            def scores(h):
                for b in range(max(2, TT * h), TT * (h + 1)):
                    s = score[b][:, :]
                    for i in range(IDX_HEADS):
                        g = "CD"[i % 2]
                        w = vw[:, b, 64 + i:65 + i]
                        r = (relu_short, relu)[h][:, i % 2, 0:NK[b]]
                        eng.wait_ge(sems["relu_ready"], st.seen("relu_ready"))
                        if i == 0:
                            ins = ts(s, r, w, 0.0, MUL, ADD)
                        else:
                            ins = stt(s, r, w, s, MUL, ADD)
                        link(ins)
                        eng.sem_inc(sems[f"{g}_free"], 1)
                        eng.sem_inc(sems["relu_used"], 1)
                        if b >= 6:
                            rounds(4, 1)
                    last = score[b][:, NK[b] - P:NK[b]]
                    link(tt(last, last, table("noncausal"), ADD))

            def rounds(b, n):
                s = score[b][:, :]
                for r in range(n):
                    eng.max(out=top8[:, :], in_=s).then_inc(sems["round_step"], 1)
                    eng.wait_ge(sems["round_step"], 2 * r + 1)
                    eng.match_replace(out=s, in_to_replace=top8[:, :], in_values=s, imm_value=TAKEN).then_inc(
                        sems["round_step"], 1)
                    eng.wait_ge(sems["round_step"], 2 * r + 2)
                eng.sem_inc(sems["round_step"], -2 * n)

            def mask(b):
                m = score[b][:, :].bitcast(BF16).rearrange("p (k two) -> p k two", two=2)[:, :, 0]
                link(ts(m, score[b][:, :], TAKEN, MASKED, ALU.not_equal, MUL))
                eng.sem_inc(sems["mask_ready"], 1)

            def topk_early():
                for b in (2, 3):
                    with st.loop(TOPK // 64):
                        rounds(b, 8)
                    mask(b)

            def retention(h, gain):
                eng.wait_ge(sems["qk_in"], st.seen("qk_in"))
                qk = r_in[:, :, 0:2, :].rearrange("p t a (h e) -> p t (a h) e", e=64)
                ro = rot[:, :, :, :].rearrange("p t a (h e) -> p t (a h) e", e=64)
                x1, x2 = qk[:, :, :, 0:32], qk[:, :, :, 32:64]
                o1, o2 = ro[:, :, :, 0:32], ro[:, :, :, 32:64]
                shape = [P, TT, 8, 32]

                def trig(name):
                    t = table(name).rearrange("p (t e) -> p t e", e=32)[:, TT * h:TT * (h + 1), :]
                    return t.unsqueeze(2).broadcast_to(shape)

                ta = rtmp[:, 0, :].rearrange("p (t a e) -> p t a e", t=TT, a=8)
                tb = rtmp[:, 1, :].rearrange("p (t a e) -> p t a e", t=TT, a=8)
                tt(ta, x1, trig("cos"), MUL)
                link(tt(tb, x2, trig("sin"), MUL))
                link(tt(o1, ta, tb, SUB))
                tt(ta, x2, trig("cos"), MUL)
                link(tt(tb, x1, trig("sin"), MUL))
                link(tt(o2, ta, tb, ADD))
                eng.sem_inc(sems["rot_ready"], 1)
                kw = r_in[:, :, 1, :].rearrange("p t (h e) -> p t h e", e=64)
                rk = rot[:, :, 1, :].rearrange("p t (h e) -> p t h e", e=64)
                wk = table("wk").unsqueeze(1).unsqueeze(3).broadcast_to([P, TT, RH, 64])
                tt(kw, rk, wk, MUL)
                if h == 0:
                    normalise(x_T, gain, rstd[:, :], 0, 2)
                eng.wait_ge(sems["rT_ready"], st.seen("rT_ready"))
                qs = rtmp[:, 0, :].rearrange("p (a c i) -> p a c i", a=2, c=TT)
                rq = rqT[:, :, :].rearrange("p a (c i) -> p a c i", c=TT)
                wq = table("wq").rearrange("p (a i) -> p a i", a=2).unsqueeze(2).broadcast_to([P, 2, TT, P])
                link(tt(qs, rq, wq, MUL))
                if h == 0:
                    link(eng.memset(state[:, 0, :, :], 0.0))
                eng.sem_inc(sems["qs_ready"], 1)
                dec = table("decay").rearrange("p (a r i) -> p a r i", a=2, r=2)
                for c in range(TT):
                    inner = rtmp[:, 1, (c % 2) * 512:(c % 2) * 512 + 512].rearrange(
                        "p (a r i) -> p a r i", a=2, r=2)
                    for r, g in enumerate("EF"):
                        eng.wait_ge(sems[f"{g}_to_dve"], st.seen(f"{g}_to_dve"))
                        link(tt(inner[:, :, r, :], bank(g, 0, 256).rearrange("p (a i) -> p a i", a=2),
                                   dec[:, :, r, :], MUL))
                        eng.sem_inc(sems[f"{g}_free"], 1)
                    eng.sem_inc(sems["st_ready"], 1)
                    if h == 0:
                        normalise(x_T, gain, rstd[:, :], *NORM_STEPS[c])
                    eng.wait_ge(sems["A_to_dve"], st.seen("A_to_dve"))
                    for a in range(2):
                        o, _ = at["gchunk"]
                        ins = stt(state[:, (c + 1) % 2, a, :], state[:, c % 2, a, :], cst[:, o + a:o + a + 1],
                                  bank("A", a * 64, a * 64 + 64), MUL, ADD)
                    link(ins)
                    eng.sem_inc(sems["A_free"], 1)
                    eng.sem_inc(sems["state_ready"], 1)
                eng.wait_ge(sems["ret_in"], st.seen("ret_in"))
                eng.wait_ge(sems["o_ready"], st.seen("o_ready"))
                o = r_in[:, :, 0, :].rearrange("p t (h e) -> p t h e", e=64)
                sqr = rot[:, :, 0, :].rearrange("p t (h e) -> p t h e", e=64)

                def stat(i):
                    return gsum[:, i, :].rearrange("p (t h) -> p t h", t=TT)

                def spread(i):
                    return stat(i).unsqueeze(3).broadcast_to([P, TT, RH, 64])

                link(eng.tensor_reduce(stat(0), o, AX_X, ADD))
                link(ts(gsum[:, 1, :], gsum[:, 0, :], 1.0 / 64, None, MUL))
                link(tt(o, o, spread(1), SUB))
                link(tt(sqr, o, o, MUL))
                link(eng.tensor_reduce(stat(3), sqr, AX_X, ADD))
                link(ts(gsum[:, 3, :], gsum[:, 3, :], 1.0 / 64, EPS, MUL, ADD))
                link(eng.reciprocal(gsum[:, 2, :], gsum[:, 3, :]))
                eng.sem_inc(sems["gvar_ready"], 1)
                if h == 1:
                    for c in range(2):
                        link(eng.memset(Z[:, c, :, :, :], 0.0))
                eng.wait_ge(sems["gstd_ready"], st.seen("gstd_ready"))
                link(tt(o, o, spread(2), MUL))
                flat = r_in[:, :, 0, :]
                link(tt(flat, flat, gn_row[:, :].unsqueeze(1).broadcast_to([P, TT, 256]), MUL))
                eng.wait_ge(sems["silu_ready"], st.seen("silu_ready"))
                link(tt(flat, flat, r_in[:, :, 3, :], MUL))
                eng.sem_inc(sems["ret_out"], 1)

            s = [s5p[:, i, :] for i in range(64)]
            ar, ai, _, dt, adt, ang, cosarg, mag, mag8, sin1, cos1 = s[:11]
            t1, t2, t3, t4, cr, ci, den = s[11:18]
            PR, PI = 20, 30
            RR, RI = 40, 48

            def cmul(orr, oi, xr, xi, yr, yi, a, b, c, d):
                tt(a, xr, yr, MUL)
                tt(b, xi, yi, MUL)
                tt(c, xr, yi, MUL)
                link(tt(d, xi, yr, MUL))
                tt(orr, a, b, SUB)
                link(tt(oi, c, d, ADD))

            def s5_angles():
                eng.wait_ge(sems["dt_ready"], st.seen("dt_ready"))
                tt(adt, ar, dt, MUL)
                link(tt(t1, ai, dt, MUL))
                magic = 12582912.0
                link(ts(t2, t1, 1.0 / (2 * np.pi), magic, MUL, ADD))
                link(ts(t2, t2, magic, None, SUB))
                for part in (6.28125, 0.0019350051879882812, 3.0199159819567e-07):
                    link(stt(t1, t2, -part, t1, MUL, ADD))
                link(ts(ang, t1, 3.1415925, -3.1415925, ALU.min, MAX))
                link(ts(t3, ang, -1.0, None, MUL))
                link(tt(t3, ang, t3, MAX))
                link(ts(cosarg, t3, -1.0, float(np.pi / 2), MUL, ADD))
                eng.sem_inc(sems["angle_ready"], 1)
                link(eng.memset(s5_ct[:, :, :, :], 0.0))

            def s5_outputs():
                st.add("s5_loaded", 16 * 8)
                eng.wait_ge(sems["E_to_dve"], st.seen("E_to_dve"))
                for r in range(2):
                    rows_ = slice(64 * r, 64 * r + 64)
                    src = bank("E").rearrange("p (c q r e) -> p c q r e", c=2, r=2, e=16)
                    for c, sign in ((0, 1.0), (1, -1.0)):
                        ins = ts(s5_ct[rows_, c, :, 16 * r:16 * r + 16], src[rows_, c, :, r, :], sign, None, MUL)
                link(ins)
                eng.sem_inc(sems["E_free"], 1)

            def s5_parameters():
                eng.wait_ge(sems["s5_loaded"], st.now("s5_loaded"))
                eng.wait_ge(sems["trig_ready"], st.seen("trig_ready"))
                tt(s[PR + 1], mag, cos1, MUL)
                tt(s[PI + 1], mag, sin1, MUL)
                eng.memset(s[PR], 1.0)
                eng.memset(s[PI], 0.0)
                tt(t1, ar, ar, MUL)
                link(tt(t2, ai, ai, MUL))
                link(tt(den, t1, t2, ADD))
                link(eng.reciprocal(den, den))
                link(ts(s[18], s[PR + 1], 1.0, None, SUB))
                tt(t1, s[18], ar, MUL)
                tt(t2, s[PI + 1], ai, MUL)
                tt(t3, s[PI + 1], ar, MUL)
                link(tt(t4, s[18], ai, MUL))
                tt(cr, t1, t2, ADD)
                link(tt(ci, t3, t4, SUB))
                tt(cr, cr, den, MUL)
                link(tt(ci, ci, den, MUL))
                cmul(s[PR + 2], s[PI + 2], s[PR + 1], s[PI + 1], s[PR + 1], s[PI + 1], t1, t2, t3, t4)
                for k, n in ((2, 2), (4, 4)):
                    for j in range(n):
                        cmul(s[PR + k + 1 + j], s[PI + k + 1 + j], s[PR + 1 + j], s[PI + 1 + j],
                             s[PR + k], s[PI + k], t1, t2, t3, t4)
                tt(s[RR], cos1, cos1, MUL)
                cmul(s[RR], s[RI], cos1, sin1, cos1, sin1, t1, t2, t3, t4)
                cmul(s[RR + 1], s[RI + 1], s[RR], s[RI], s[RR], s[RI], t1, t2, t3, t4)
                cmul(s[RR], s[RI], s[RR + 1], s[RI + 1], s[RR + 1], s[RI + 1], t1, t2, t3, t4)
                for k in range(6):
                    cmul(s[RR + k + 1], s[RI + k + 1], s[RR + k], s[RI + k], s[RR + k], s[RI + k],
                         t1, t2, t3, t4)
                crb, cib = (a.unsqueeze(2).broadcast_to([P, 8, 16]) for a in (cr, ci))
                br, bi = s5_b[:, 0, :, :], s5_b[:, 1, :, :]
                tt(s5_t[:, 0, :, :], crb, br, MUL)
                link(tt(s5_t[:, 1, :, :], cib, bi, MUL))
                link(tt(s5_bb[:, 0, :, :], s5_t[:, 0, :, :], s5_t[:, 1, :, :], SUB))
                tt(s5_t[:, 0, :, :], crb, bi, MUL)
                link(tt(s5_t[:, 1, :, :], cib, br, MUL))
                link(tt(s5_bb[:, 1, :, :], s5_t[:, 0, :, :], s5_t[:, 1, :, :], ADD))

            def s5():
                pw = [s5p[:, o:o + 9, :] for o in (PR, PI)]
                xa, xb = Xt[:, 0, :], Xt[:, 1, :]
                for hh in range(2):
                    qs = slice(4 * hh, 4 * hh + 4)
                    zs = [P, 8, 4, 16]
                    za, zb = (t.rearrange("p (m q e) -> p m q e", m=8, q=4) for t in (xa, xb))

                    def power(c, sl=slice(0, 8), shape=zs):
                        return pw[c][:, sl, qs].unsqueeze(3).broadcast_to(shape)

                    def inp(c):
                        return s5_bb[:, c, qs, :].unsqueeze(1).broadcast_to(zs)

                    for c in range(2):
                        tt(za, power(0), inp(c), MUL)
                        link(tt(zb, power(1), inp(1 - c), MUL))
                        for r in range(2):
                            rows_ = slice(64 * r, 64 * r + 64)
                            ins = tt(Z[rows_, c, :, :, 16 * r:16 * r + 16], za[rows_], zb[rows_],
                                     ADD if c else SUB)
                        link(ins)
                    eng.sem_inc(sems["z_ready"], 1)
                    if hh == 0:
                        eng.wait_ge(sems["retT_ready"], st.seen("retT_ready", 2))
                    else:
                        eng.wait_ge(sems["y_ready"], st.seen("y_ready"))
                    ys = [P, 4, 4, 32]
                    ya, yb = (t.rearrange("p (m q e) -> p m q e", m=4, q=4) for t in (xa, xb))
                    for m in range(2):
                        sl = slice(1 + 4 * m, 5 + 4 * m)
                        cr_, ni_ = (s5_ct[:, c, qs, :].unsqueeze(1).broadcast_to(ys) for c in range(2))
                        tt(ya, power(0, sl, ys), cr_, MUL)
                        link(tt(yb, power(1, sl, ys), ni_, MUL))
                        flat = [Yt[:, c, 4 * m:4 * m + 4, :, :].rearrange("p m q e -> p (m q e)")
                                for c in range(2)]
                        link(tt(flat[0], xa, xb, ADD))
                        tt(ya, power(1, sl, ys), cr_, MUL)
                        link(tt(yb, power(0, sl, ys), ni_, MUL))
                        link(tt(flat[1], xb, xa, SUB))
                    for a, g in enumerate("EF"):
                        eng.wait_ge(sems[f"{g}_to_dve"], st.seen(f"{g}_to_dve"))
                        link(tt(Kt[:, 4 * a:4 * a + 4, :], bank(g).rearrange("p (m o) -> p m o", m=4),
                                   table("quads").unsqueeze(1).broadcast_to([P, 4, P]), MUL))
                        eng.sem_inc(sems[f"{g}_free"], 1)
                    link(stt(Kt[:, 0, :], ident, s5_col[:, 0, hh:hh + 1], Kt[:, 0, :], MUL, ADD))
                    eng.sem_inc(sems["kt_ready"], 1)
                    eng.memset(Et[:, 0, :, 0:1], 1.0)
                    link(eng.memset(Et[:, 1, :, 0:1], 0.0))
                    for k in range(7):
                        n = 1 << k
                        sh = [P, 4, n]
                        rr, ri = (s5p[:, o + k, qs].unsqueeze(2).broadcast_to(sh) for o in (RR, RI))
                        tmp = [Xt[:, i // 2, (i % 2) * 256:(i % 2) * 256 + 4 * n].rearrange(
                            "p (q c) -> p q c", q=4) for i in range(4)]
                        cmul(Et[:, 0, :, n:2 * n], Et[:, 1, :, n:2 * n], Et[:, 0, :, 0:n], Et[:, 1, :, 0:n],
                             rr, ri, *tmp)
                    def flat4(t, c):
                        return t[:, c, :, :].rearrange("p q c -> p (q c)")

                    er, ei = flat4(Et, 0), flat4(Et, 1)
                    eng.wait_ge(sems["v_ready"], st.seen("v_ready"))
                    hr, hi = flat4(Ht, 0), flat4(Ht, 1)
                    gr, gi = flat4(Gt, 0), flat4(Gt, 1)
                    tt(xa, er, hr, MUL)
                    link(tt(xb, ei, hi, MUL))
                    link(tt(gr, xa, xb, ADD))
                    tt(xa, er, hi, MUL)
                    link(tt(xb, ei, hr, MUL))
                    link(tt(gi, xa, xb, SUB))
                    for c in range(2):
                        for q in range(4):
                            decay = mag8[:, 4 * hh + q:4 * hh + q + 1].broadcast_to([P, P])
                            ins = eng.tensor_tensor_scan(Ht[:, c, q, :], decay, Gt[:, c, q, :], 0.0,
                                                         op0=MUL, op1=ADD)
                    link(ins)
                    tt(xa, er, hr, MUL)
                    link(tt(xb, ei, hi, MUL))
                    x4 = [t.rearrange("p (q c) -> p q c", q=4)[:, :, 0:P - 1] for t in (xa, xb)]
                    eng.memset(Gt[:, 0, :, 0:1], 0.0)
                    eng.memset(Gt[:, 1, :, 0:1], 0.0)
                    link(tt(Gt[:, 0, :, 1:P], x4[0], x4[1], SUB))
                    tt(xa, er, hi, MUL)
                    link(tt(xb, ei, hr, MUL))
                    link(tt(Gt[:, 1, :, 1:P], x4[0], x4[1], ADD))
                    eng.sem_inc(sems["hprev_ready"], 1)
                st.add("y_ready")
                eng.wait_ge(sems["sig_ready"], st.seen("sig_ready"))
                z2 = Z[:, :, :, :, :].rearrange("p a m q r -> p (a m q r)").rearrange("p (m t) -> p m t", m=2)
                link(tt(cm[:, 0:2, :], cm[:, 0:2, :], z2, MUL))
                eng.sem_inc(sems["y_gated"], 1)

            def attend(h):
                for b in range(TT * h, TT * (h + 1)):
                    nk = NK[b]
                    win = min(256, nk)

                    def copies(i):
                        if b >= 4 or i % 2 == 1:
                            eng.wait_ge(sems["B_to_dve"], st.seen("B_to_dve"))
                            lo, n = (512, nk - 512) if b >= 4 else (0, nk)
                            eng.tensor_copy(probT[:, i % 2, lo:lo + n],
                                                                   bank("B", 0, n)).then_inc(sems["ptB_ready"], st.made("ptB_ready"))

                    for i in range(HEADS):
                        g = "CD"[i % 2]
                        eng.wait_ge(sems[f"{g}_to_dve"], st.seen(f"{g}_to_dve"))
                        near = bank(g, nk - win, nk)
                        link(tt(near, near, bias_win[:, i, 256 - win:256], ADD))
                        eng.tensor_reduce(nmax[:, i:i + 1], bank(g, 0, nk), AX_X,
                                                                  MAX, negate=True).then_inc(sems["nmax_ready"], st.made("nmax_ready"))
                        if i >= 1:
                            copies(i - 1)
                        if h == 0 and (b >= 2 or i % 2):
                            rounds(4 if b >= 2 else 5, 1)
                    copies(HEADS - 1)
                    eng.wait_ge(sems["E_to_dve"], st.seen("E_to_dve"))
                    link(eng.reciprocal(rinv[:, :], rsum[:, :]))
                    link(tt(ao[:, :].rearrange("p (h e) -> p h e", h=HEADS),
                               bank("E").rearrange("p (h e) -> p h e", h=HEADS),
                               rinv[:, :].unsqueeze(2).broadcast_to([P, HEADS, DH]), MUL))
                    eng.sem_inc(sems["E_free"], 1)
                    eng.sem_inc(sems["ao_ready"], 1)
                    eng.wait_ge(sems["mix_hi_ready"], st.seen("mix_hi_ready"))
                    o = (b % TT) * P
                    link(tt(h_lo[:, 2:6, o:o + P], bank("F").rearrange("p (a c) -> p a c", a=4),
                               h_hi[:, 2:6, o:o + P].bitcast(F32), SUB))
                    eng.sem_inc(sems["F_free"], 1)
                    eng.sem_inc(sems["mix_ready"], 1)
                    if b % TT == 0:
                        eng.wait_ge(sems["mix_hi_ready"], st.seen("mix_hi_ready"))
                        cols = slice(h * HALF, (h + 1) * HALF)
                        tt(h_lo[:, 0:2, :], cm[:, 0:2, cols], h_hi[:, 0:2, :].bitcast(F32), SUB)
                        tt(h_lo[:, 6:8, :], ret_T[:, :, cols], h_hi[:, 6:8, :].bitcast(F32), SUB).then_inc(sems["mix_ready"], st.made("mix_ready"))

            def mix_out(h, gain):
                if h == 0:
                    st.add("unit_done", 2 * UNITS_PROJ)
                eng.wait_ge(sems["x_loaded"], st.seen("x_loaded", 16))
                clear_sum()
                with st.loop(4, unit_done=2, dve_chain=4, square_ready=2) as i:
                    for e, g in enumerate("AB"):
                        if h == 0:
                            hold()
                            rounds(4, 1)
                        eng.wait_ge(sems["unit_done"], st.seen("unit_done"))
                        xk = x_T[:, ds(i * 2 + e, 1), :].rearrange("p o c -> p (o c)")
                        link(tt(xk, xk, bank(g), ADD))
                        eng.sem_inc(sems[f"{g}_free"], 1)
                        eng.sem_inc(sems["x_updated"], 1)
                        add_squares()
                rsqrt()
                factors(keep=False)
                normalise(x_T, gain, bank("F"))
                eng.wait_ge(sems["norm_tmp"], st.now("norm_tmp"))
                eng.sem_inc(sems["F_free"], 1)

            def ffn(l, h):
                selected = {4: TOPK // 8, 5: 8, 6: 0, 7: 0} if h == 0 else {}
                for c, n in enumerate(FF_CHUNKS):
                    step, after = EARLY[c] if h == 0 else ((), ())
                    last_chunk = c == len(FF_CHUNKS) - 1
                    sums = h == 1 and c == 1
                    if sums:
                        clear_sum()
                    def tile_of(t, i):
                        return t[:, i, :] if isinstance(i, int) else t[:, ds(i, 1), :].rearrange("p o c -> p (o c)")

                    def gated(i):
                        st.add("unit_done")
                        eng.wait_ge(sems["gate_ready"], st.seen("gate_ready"))
                        eng.wait_ge(sems["unit_done"], st.seen("unit_done"))
                        link(tt(atmp[:, :], bank("B"), gate[:, :], MUL))
                        eng.sem_inc(sems["B_free"], 1)
                        eng.sem_inc(sems["gate_used"], 1)
                        hi = tile_of(a_hi, i)
                        lo = tile_of(a_lo, i)
                        link(eng.tensor_copy(hi, atmp[:, :]))
                        tt(lo, atmp[:, :], hi.bitcast(F32), SUB).then_inc(sems["a_ready"], st.made("a_ready"))
                        if sums:
                            add_squares()
                        eng.wait_ge(sems["a_ready"], st.now("a_ready"))
                        if step:
                            hold()
                        for b, k in step:
                            rounds(b, k)

                    early_mean = h == 1 and last_chunk
                    with st.loop(n - early_mean, unit_done=2, gate_ready=1, dve_chain=2 + int(sums), a_ready=1,
                                 square_ready=int(sums)) as i:
                        gated(i)
                    if early_mean:
                        rsqrt()
                        gated(n - 1)
                    for b, k in step:
                        selected[b] += n * k
                    for b, k in after:
                        rounds(b, k)
                        selected[b] += k
                    for b, k in selected.items():
                        if k == TOPK // 8:
                            mask(b)
                            selected[b] = 0
                    if early_mean:
                        factors()
                        if l + 1 < DEPTH:
                            normalise(x_next, l + 1, rstd[:, :])
                        else:
                            scale_last(x_next)
                    st.add("unit_done", n)
                    for g, (first, k) in GROUPS.items():
                        if g == "F":
                            eng.wait_ge(sems["unit_done"], st.now("unit_done"))
                        else:
                            eng.wait_ge(sems[f"{g}_to_dve"], st.seen(f"{g}_to_dve"))
                        xk = x_T[:, first:first + k, :].rearrange("p k c -> p (k c)")
                        link(tt(xk, xk, bank(g), ADD))
                        eng.sem_inc(sems[f"{g}_free"], 1)
                eng.sem_inc(sems["x_updated"], 1)

            eng.wait_ge(sems["const_loaded"], 80)
            ts(causal_b[:, :], table("noncausal"), MASKED / NONCAUSAL, None, MUL).then_inc(sems["ident_ready"], st.made("ident_ready"))
            clear_sum()
            for t in range(NB):
                g = "CD"[t % 2]
                eng.wait_ge(sems[f"{g}_to_dve"], st.seen(f"{g}_to_dve"))
                c = (t % TT) * P
                link(eng.tensor_copy((x_next, x_T)[t // TT][:, :, c:c + P],
                                     bank(g).rearrange("p (k c) -> p k c", k=KT)))
                eng.sem_inc(sems[f"{g}_free"], 1)
                eng.sem_inc(sems["xtok_used"], 1)
                if t % TT == TT - 1:
                    eng.sem_inc(sems["x_updated"], 1)
            for k in range(KT):
                add_squares()
            rsqrt()
            factors()
            normalise(x_next, 0, rstd[:, :])
            for l in range(DEPTH):
                clear_sum()
                s5_angles()
                for k in range(KT):
                    if k == 2:
                        s5_outputs()
                    add_squares()
                rsqrt()
                factors()
                s5_parameters()
                retention(0, l)
                scores(0)
                topk_early()
                retention(1, l)
                s5()
                scores(1)
                attend(0)
                mix_out(0, DEPTH + l)
                ffn(l, 0)
                attend(1)
                mix_out(1, DEPTH + l)
                ffn(l, 1)
            clear_sum()
            for k in range(KT):
                add_squares()
            for h in range(2):
                if h == 1:
                    rsqrt()
                    factors()
                    scale_last(x_T)
                for t in range(TT):
                    g = "CD"[t % 2]
                    eng.wait_ge(sems[f"{g}_to_dve"], st.seen(f"{g}_to_dve"))
                    if h * TT + t >= 2:
                        eng.wait_ge(sems[f"out_stored{t % 2}"], st.seen(f"out_stored{t % 2}", 16))
                    link(eng.tensor_copy(xtok[:, t % 2, :], bank(g)))
                    eng.sem_inc(sems[f"{g}_free"], 1)
                    eng.sem_inc(sems["fin_out"], 1)

        @block.tensor
        def _(eng):
            st = Counts(eng, "pe", sems["pe_held"])

            def mm(out_, lhsT, rhs, start, stop):
                return eng.matmul(out_, lhsT, rhs, start=start, stop=stop, skip_group_check=True)

            def take(*groups):
                for g in groups:
                    eng.wait_ge(sems[f"{g}_free"], st.taken(f"{g}_free"))

            def give(g, to, ins):
                ins.then_inc(sems[f"{g}_to_{to}"], st.made(f"{g}_to_{to}"))

            PARTS = ((w_hi, 0), (w_hi, 1), (w_lo, 0))

            def token_sums():
                eng.wait_ge(sems["sum_ready"], st.seen("sum_ready"))
                take("F")
                for t in range(TT):
                    ins = mm(bank("F", t, t + 1), rstd[:, t * P:(t + 1) * P], table("ones")[:, 0:1], True, True)
                give("F", "dve", ins)

            def spread():
                eng.wait_ge(sems["diag_ready"], st.seen("diag_ready"))
                give("F", "dve", mm(bank("F"), table("ones"), rstd[:, :], True, True))

            def mean():
                token_sums()
                spread()

            def unit(g, first=False):
                slot = st.count.get("weights_ready", 0) % 2
                eng.wait_ge(sems["weights_ready"], st.seen("weights_ready"))
                take(g)
                for k in range(KT):
                    if first:
                        eng.wait_ge(sems["h_ready"], st.seen("h_ready"))
                    for j, (w, part) in enumerate(PARTS):
                        ins = mm(bank(g), w[:, slot, k * P:(k + 1) * P], (h_hi, h_lo)[part][:, k, :],
                                 k == 0 and j == 0, k == KT - 1 and j == 2)
                ins.then_inc(sems["unit_done"], st.made("unit_done"))

            def units(times, normed=True):
                if normed:
                    unit("A", first=True)
                    unit("B")
                with st.loop(times - normed, weights_ready=2, unit_done=2, A_free=1, B_free=1):
                    unit("A")
                    unit("B")

            def s5_outputs():
                take("E")
                eng.wait_ge(sems["s5_loaded"], st.seen("s5_loaded", 16 * 8))
                for c in range(2):
                    for hh in range(2):
                        o = (2 * c + hh) * P
                        ins = eng.transpose(bank("E", o, o + P), s5_c[:, c, hh, :], ident)
                give("E", "dve", ins)

            def token_mms(out_, t, k, w, start, stop):
                cols = slice(t * P, (t + 1) * P)
                parts = ((h_hi, 0), (h_hi, 1), (h_lo, 0))
                for j, (x_, part) in enumerate(parts):
                    ins = mm(out_, x_[:, k, cols], w[part], start and j == 0, stop and j == 2)
                return ins

            def proj(h):
                if h == 0:
                    unit("A", first=True)
                    unit("B")
                    s5_outputs()
                    units(4, normed=False)
                    token_sums()
                else:
                    units(4, normed=False)
                slot = st.count["weights_ready"] % 2
                eng.wait_ge(sems["weights_ready"], st.seen("weights_ready"))
                take("E")
                for t in range(TT):
                    for k in range(KT):
                        w = [x_[:, slot, k * P:(k + 1) * P] for x_ in (w_hi, w_lo)]
                        ins = token_mms(bank("E", t * P, (t + 1) * P), t, k, w, k == 0, k == KT - 1)
                ins.then_inc(sems["unit_done"], st.made("unit_done"))
                if h == 0:
                    spread()
                for n in range(2):
                    if n == 0:
                        take("C", "D")
                        outs = [bank("C", 0, 512), bank("C", 512, 1024), bank("D", 0, 512), bank("D", 512, 1024)]
                    else:
                        take("E", "F", "A", "B")
                        outs = [bank(g) for g in "EFAB"]
                    for j in range(4):
                        slot = st.count["weights_ready"] % 2
                        eng.wait_ge(sems["weights_ready"], st.seen("weights_ready"))
                        for t in range(TT):
                            for k in range(2):
                                w = [x_[:, slot, k * 512:(k + 1) * 512] for x_ in (w_hi, w_lo)]
                                ins = token_mms(outs[t], t, 2 * j + k, w, j == 0 and k == 0,
                                                j == 3 and k == 1)
                        ins.then_inc(sems["unit_done"], st.made("unit_done"))

            def scores(h):
                eng.wait_ge(sems["cm_ready"], st.seen("cm_ready"))
                for b in range(max(2, TT * h), TT * (h + 1)):
                    q = slice((b % TT) * P, (b % TT + 1) * P)
                    for i in range(IDX_HEADS):
                        g = "CD"[i % 2]
                        r = slice(64 * (i % 2), 64 * (i % 2) + 64)
                        take(g)
                        for a in range(0, NK[b], 512):
                            n = min(512, NK[b] - a)
                            ins = mm(bank(g, a, a + n), iq[r, i // 2, q], cm[r, 7, a:a + n], True, True)
                        give(g, "act", ins)

            def retention(h):
                eng.wait_ge(sems["rot_ready"], st.seen("rot_ready"))
                take("A", "B", "C")
                for a in range(2):
                    for t in range(TT):
                        ins = eng.transpose(bank("AB"[a], t * P, (t + 1) * P),
                                            rot[:, t, 0, a * P:(a + 1) * P], ident)
                    give("AB"[a], "act", ins)
                for a in range(2):
                    for t in range(TT):
                        ins = eng.transpose(bank("C", a * 512 + t * P, a * 512 + (t + 1) * P),
                                            rot[:, t, 1, a * P:(a + 1) * P], ident)
                give("C", "act", ins)
                eng.wait_ge(sems["qs_ready"], st.seen("qs_ready"))
                eng.wait_ge(sems["ret_in"], st.seen("ret_in"))
                qs = rtmp[:, 0, :].rearrange("p (a c i) -> p a c i", a=2, c=TT)
                for c in range(TT):
                    cols = slice(c * P, (c + 1) * P)
                    for r, g in enumerate("EF"):
                        half = slice(64 * r, 64 * r + 64)
                        take(g)
                        for a in range(2):
                            ins = mm(bank(g, a * P, (a + 1) * P), rkT[half, a, cols], rqT[half, a, cols],
                                     True, True)
                        give(g, "dve", ins)
                    inner = rtmp[:, 1, (c % 2) * 512:(c % 2) * 512 + 512].rearrange(
                        "p (a r i) -> p a r i", a=2, r=2)
                    eng.wait_ge(sems["st_ready"], st.seen("st_ready"))
                    if c:
                        eng.wait_ge(sems["state_ready"], st.seen("state_ready"))
                    take("D")
                    for r in range(2):
                        half = slice(64 * r, 64 * r + 64)
                        for a in range(2):
                            hd = 2 * a + r
                            o = bank("D", 512 * r + a * 64, 512 * r + a * 64 + 64)
                            mm(o, inner[:, a, r, :], r_in[:, c, 2, 64 * hd:64 * hd + 64], True, False)
                            ins = mm(o, qs[half, a, c, :], state[half, c % 2, a, :], False, True)
                    give("D", "act", ins)
                    take("A")
                    for r in range(2):
                        for a in range(2):
                            hd = 2 * a + r
                            ins = mm(bank("A", a * 64, a * 64 + 64)[64 * r:64 * r + 64, :],
                                     r_in[:, c, 1, 64 * hd:64 * hd + 64],
                                     r_in[:, c, 2, 64 * hd:64 * hd + 64], True, True)
                    give("A", "dve", ins)
                eng.wait_ge(sems["state_ready"], st.seen("state_ready"))
                if h == 0:
                    unit("A", first=True)
                    unit("B")
                eng.wait_ge(sems["ret_out"], st.seen("ret_out"))
                take("C")
                for a in range(2):
                    for t in range(TT):
                        ins = eng.transpose(bank("C", a * 512 + t * P, a * 512 + (t + 1) * P),
                                            r_in[:, t, 0, a * P:(a + 1) * P], ident)
                give("C", "act", ins)

            def s5():
                for hh in range(2):
                    u = cm[:, hh, :].rearrange("p (c j) -> p j c", j=8)
                    eng.wait_ge(sems["z_ready"], st.seen("z_ready"))
                    for c, g in enumerate("CD"):
                        take(g)
                        for m in range(8):
                            ins = eng.transpose(bank(g, m * P, (m + 1) * P),
                                                Z[:, c, m, :, :].rearrange("p q e -> p (q e)"), ident)
                        give(g, "act", ins)
                    for a, g in enumerate("EF"):
                        take(g)
                        for m in range(4 * a, 4 * a + 4):
                            o = (m % 4) * P
                            for c in range(2):
                                ins = mm(bank(g, o, o + P), Z[:, c, m, :, :].rearrange("p q e -> p (q e)"),
                                         s5_ct[:, c, 4 * hh:4 * hh + 4, :].rearrange("p q e -> p (q e)"),
                                         c == 0, c == 1)
                        give(g, "dve", ins)
                    eng.wait_ge(sems["vt_ready"], st.seen("vt_ready"))
                    for q, g in enumerate("ABCD"):
                        take(g)
                        rows_ = slice(32 * q, 32 * q + 32)
                        for c in range(2):
                            for j in range(8):
                                ins = mm(bank(g, c * P, (c + 1) * P), Vt[rows_, 7 - j, c, :], u[rows_, j, :],
                                         j == 0, j == 7)
                        give(g, "act", ins)
                    eng.wait_ge(sems["kt_ready"], st.seen("kt_ready"))
                    take("C")
                    for j in range(8):
                        for i in range(j + 1):
                            mm(bank("C", j * P, (j + 1) * P), Kt[:, j - i, :], u[:, i, :], j % 4 == 0 and i == 0, False)
                    eng.wait_ge(sems["hprev_ready"], st.seen("hprev_ready"))
                    for j in range(8):
                        o = bank("C", j * P, (j + 1) * P)
                        for q in range(4):
                            for c in range(2):
                                ins = mm(o[32 * q:32 * q + 32, :], Yt[:, c, j, q, :], Gt[:, c, q, :], False, c == 1)
                    give("C", "act", ins)
                eng.wait_ge(sems["y_ready"], st.seen("y_ready", 2))
                for n in range(2):
                    for m in range(2):
                        g = "EFAB"[2 * n + m]
                        take(g)
                        for k in range(2):
                            ins = mm(bank(g), s5_glu[:, k, m * P:(m + 1) * P],
                                     cm[:, k, n * HALF:(n + 1) * HALF], k == 0, k == 1)
                        give(g, "act", ins)

            def attend(h):
                masks = range(2, 4) if h == 0 else range(4, NB)
                eng.wait_ge(sems["mask_ready"], st.seen("mask_ready", len(masks)))
                for b in range(TT * h, TT * (h + 1)):
                    nk, q = NK[b], slice(b * P, (b + 1) * P)
                    if b >= 2:
                        m = score[b][:, :].bitcast(BF16).rearrange("p (k two) -> p k two", two=2)[:, :, 0]

                    def logits(i):
                        g = "CD"[i % 2]
                        r = slice(64 * (i % 2), 64 * (i % 2) + 64)
                        take(g)
                        for a in range(0, nk, 512):
                            n = min(512, nk - a)
                            mm(bank(g, a, a + n), cm[r, CM_Q + i // 2, q], cm[r, 6, a:a + n], True, False)
                            if b >= 2:
                                ins = mm(bank(g, a, a + n), ident_b[:, :], m[:, a:a + n], False, True)
                            else:
                                ins = mm(bank(g, nk - P, nk), ident_b[:, :], causal_b[:, :], False, True)
                        give(g, "dve", ins)

                    def turn(i):
                        eng.wait_ge(sems["p_ready"], st.seen("p_ready"))
                        eng.sem_inc(sems["CD"[i % 2] + "_free"], 1)
                        if i:
                            turned(i - 1)
                        if b >= 4:
                            parts = (("A", 0, 4, "act"), ("B", 4, b + 1, "dve"))
                        else:
                            parts = ((("A", 0, b + 1, "act"), ("B", 0, b + 1, "dve"))[i % 2],)
                        for g, k0, k1, to in parts:
                            take(g)
                            for k in range(k0, k1):
                                ins = eng.transpose(bank(g, (k - k0) * P, (k - k0 + 1) * P),
                                                    prob[:, i % 2, k * P:(k + 1) * P], ident)
                            give(g, to, ins)

                    def turned(i):
                        if b >= 4 or i % 2 == 0:
                            eng.wait_ge(sems["ptA_ready"], st.seen("ptA_ready"))
                            eng.sem_inc(sems["A_free"], 1)
                        if b >= 4 or i % 2 == 1:
                            eng.wait_ge(sems["ptB_ready"], st.seen("ptB_ready"))
                            eng.sem_inc(sems["B_free"], 1)

                    def values(i):
                        for k in range(b + 1):
                            ins = mm(bank("E", i * DH, (i + 1) * DH), probT[:, i % 2, k * P:(k + 1) * P],
                                     vw[:, k, 0:DH], k == 0, k == b)
                        return ins

                    take("E")
                    logits(0)
                    logits(1)
                    for i in range(HEADS):
                        turn(i)
                        if i + 2 < HEADS:
                            logits(i + 2)
                        if i >= 1:
                            values(i - 1)
                    turned(HEADS - 1)
                    give("E", "dve", values(HEADS - 1))
                    eng.wait_ge(sems["ao_ready"], st.seen("ao_ready"))
                    take("F")
                    for a in range(4):
                        ins = eng.transpose(bank("F", a * P, (a + 1) * P), ao[:, a * P:(a + 1) * P], ident)
                    give("F", "act", ins)

            def ffn(h):
                for c, n in enumerate(FF_CHUNKS):
                    if h == 1 and c == len(FF_CHUNKS) - 1:
                        units(n - 1, normed=False)
                        token_sums()
                        unit("A")
                        unit("B")
                        spread()
                    else:
                        units(n, normed=c == 0)
                    eng.wait_ge(sems["a_ready"], st.seen("a_ready", n - 1))

                    def down(f, first=False, last=False):
                        slot = st.count["weights_ready"] % 2
                        eng.wait_ge(sems["weights_ready"], st.seen("weights_ready"))
                        for m in (2, 3, 4, 5, 6, 7, 0, 1) if first else range(KT):
                            start = [g for g, (bank0, _) in GROUPS.items() if bank0 == m]
                            end = [g for g, (bank0, k) in GROUPS.items() if bank0 + k - 1 == m]
                            if first:
                                take(*start)
                            for j, (w, part) in enumerate(PARTS):
                                src = (a_hi, a_lo)[part]
                                rhs = src[:, f, :] if isinstance(f, int) else src[:, ds(f, 1), :].rearrange(
                                    "p o c -> p (o c)")
                                ins = mm(psum[:, m * 512:(m + 1) * 512], w[:, slot, m * P:(m + 1) * P], rhs,
                                         first and j == 0, last and j == 2)
                            if last and end and m < KT - 1:
                                give(end[0], "dve", ins)
                        ins.then_inc(sems["unit_done"], st.made("unit_done"))

                    down(0, first=True)
                    down(1)
                    with st.loop(n // 2 - 2, weights_ready=2, unit_done=2) as i:
                        down(i * 2 + 2)
                        down(i * 2 + 3)
                    down(n - 2)
                    eng.wait_ge(sems["a_ready"], st.seen("a_ready"))
                    down(n - 1, last=True)

            eng.wait_ge(sems["const_loaded"], 80)
            for name, n in CREDIT.items():
                eng.sem_inc(sems[name], n)
            take("E")
            give("E", "act", mm(bank("E", 0, 384)[0:HEADS, :], rel_b[:, :],
                                table("buckets")[0:BUCKETS, :], True, True))
            for t in range(NB):
                g = "CD"[t % 2]
                eng.wait_ge(sems[f"xtok_loaded{t % 2}"], st.seen(f"xtok_loaded{t % 2}", 16))
                take(g)
                for k in range(KT):
                    ins = eng.transpose(bank(g, k * P, (k + 1) * P), xtok[:, t % 2, k * P:(k + 1) * P], ident)
                give(g, "dve", ins)
            eng.wait_ge(sems["ident_ready"], st.seen("ident_ready", 2))
            mean()
            for l in range(DEPTH):
                proj(0)
                retention(0)
                scores(0)
                proj(1)
                retention(1)
                s5()
                scores(1)
                for h in range(2):
                    attend(h)
                    eng.wait_ge(sems["mix_ready"], st.seen("mix_ready", TT + 1))
                    units(4, normed=False)
                    mean()
                    ffn(h)
            for h in range(2):
                if h == 1:
                    mean()
                eng.wait_ge(sems["fin_ready"], st.seen("fin_ready"))
                x_half = (x_next, x_T)[h]
                for t in range(TT):
                    g = "CD"[t % 2]
                    take(g)
                    for k in range(KT):
                        ins = eng.transpose(bank(g, k * P, (k + 1) * P), x_half[:, k, t * P:(t + 1) * P], ident)
                    give(g, "dve", ins)


_INS = ['x', 'w_in', 'w_out', 'norm_mix', 'ssm_a_re', 'ssm_a_im', 'ssm_log_dt', 'ssm_b_re', 'ssm_b_im',
        'ssm_c_re', 'ssm_c_im', 'ssm_d', 'ssm_glu_w', 'ssm_glu_b', 'rel_bias', 'ret_gn', 'norm_ffn',
        'w_ffn_in', 'w_ffn_out', 'norm_final']


def kernel(**inputs):
    import numpy as _np
    import concourse.bacc as _bacc
    from concourse import mybir as _mybir
    from concourse.bass_utils import run_bass_kernel_spmd as _run

    nc = _bacc.Bacc("TRN2", target_bir_lowering=False, num_devices=1)
    arrays, args = {}, []
    for name in _INS:
        a = _np.ascontiguousarray(inputs[name])
        arrays[f"in_{name}_dram"] = a
        args.append(nc.dram_tensor(f"in_{name}_dram", a.shape, _mybir.dt.from_np(a.dtype), kind="ExternalInput").ap())
    tables, at = constants()
    arrays["tables_dram"] = tables
    args.append(nc.dram_tensor("tables_dram", tables.shape, _mybir.dt.float32, kind="ExternalInput").ap())
    args.append(nc.dram_tensor("out_0_dram", (1, T, D), _mybir.dt.float32, kind="ExternalOutput").ap())
    build_trunk(nc, *args, at)
    r = _run(nc, [arrays], core_ids=[0])
    return r.results[0]["out_0_dram"]
```
